# Optimizing a Trainium2 kernel written in Bass

```python
import math
import jax, jax.numpy as jnp
from jax import lax
import numpy as np

D_MODEL = 1024
BATCH = 1
SEQ = 256
DEPTH = 1

CHUNK = 64
MIX_WIDTH = D_MODEL
POOL_WIDTH = MIX_WIDTH // 2
POOL_WINDOWS = (2, 4, 8, 16)
POOL_GROUP = POOL_WIDTH // len(POOL_WINDOWS)
ATTN_HEADS = 8
HEAD_DIM = (MIX_WIDTH - POOL_WIDTH) // ATTN_HEADS
ATTN_WIDTH = ATTN_HEADS * HEAD_DIM
IDX_HEADS = 8
IDX_DIM = 64
TOPK_MAX = 256
Q_BLOCK = 128
ROPE_THETA = 10000.0
MEM_TOKENS = 256
MEM_HEADS = 4
MEM_HEAD_DIM = 128
MEM_WIDTH = MEM_HEADS * MEM_HEAD_DIM
N_GROUPS = 4
EXPERTS_PER_GROUP = 8
EXPERT_FF = 256
TOP_K_EXPERTS = 2
EPS = 1e-6
OFF_POOL = 0
OFF_Q = OFF_POOL + POOL_WIDTH
OFF_K = OFF_Q + ATTN_WIDTH
OFF_V = OFF_K + ATTN_WIDTH
OFF_QI = OFF_V + ATTN_WIDTH
OFF_KI = OFF_QI + IDX_HEADS * IDX_DIM
OFF_WI = OFF_KI + IDX_DIM
IN_COLS = OFF_WI + IDX_HEADS


def rmsnorm(x, g):
    xf = x.astype(jnp.float32)
    y = xf * lax.rsqrt(jnp.mean(xf * xf, axis=-1, keepdims=True) + EPS)
    return (y * g.astype(jnp.float32)).astype(x.dtype)

def rope_tables(seq_len, dim):
    inv = ROPE_THETA ** (-jnp.arange(0, dim, 2, dtype=jnp.float32) / dim)
    ang = jnp.arange(seq_len, dtype=jnp.float32)[:, None] * inv[None, :]
    ang = jnp.concatenate([ang, ang], axis=-1)
    return jnp.cos(ang), jnp.sin(ang)

def apply_rope(x, cos, sin):
    xf = x.astype(jnp.float32)
    half = xf.shape[-1] // 2
    rot = jnp.concatenate([-xf[..., half:], xf[..., :half]], axis=-1)
    return (xf * cos[None, :, None, :] + rot * sin[None, :, None, :]).astype(x.dtype)

def pool_mixer(u, pool_w, pool_scale):
    B, S, _ = u.shape
    uf = u.astype(jnp.float32)
    pos1 = jnp.arange(1, S + 1)
    outs = []
    for g, w in enumerate(POOL_WINDOWS):
        ug = uf[..., g * POOL_GROUP:(g + 1) * POOL_GROUP]
        cs = jnp.cumsum(ug, axis=1)
        lag = jnp.pad(cs, ((0, 0), (w, 0), (0, 0)))[:, :S]
        cnt = jnp.minimum(pos1, w).astype(jnp.float32)[None, :, None]
        mixed = ((cs - lag) / cnt - ug).astype(u.dtype)
        outs.append(jnp.einsum('bsc,cd->bsd', mixed, pool_w[g]))
    return jnp.concatenate(outs, axis=-1) * pool_scale

def dsa_attention(q, k, v, qi, ki, wi):
    B, S, H, Dh = q.shape
    topk = min(TOPK_MAX, S // 4)
    n_blocks = S // Q_BLOCK
    key_chunk = jnp.arange(S) // CHUNK
    idx_scale = (IDX_DIM ** -0.5) * (IDX_HEADS ** -0.5)
    gather = jax.vmap(lambda a, ix: a[ix])

    def block(i):
        start = i * Q_BLOCK
        qb = lax.dynamic_slice_in_dim(q, start, Q_BLOCK, axis=1)
        qib = lax.dynamic_slice_in_dim(qi, start, Q_BLOCK, axis=1)
        wib = lax.dynamic_slice_in_dim(wi, start, Q_BLOCK, axis=1)
        q_chunk = (start + jnp.arange(Q_BLOCK)) // CHUNK
        adm = key_chunk[None, :] <= q_chunk[:, None]
        rel = jax.nn.relu(jnp.einsum('bthd,bsd->bths', qib, ki).astype(jnp.float32))
        score = jnp.einsum('bths,bth->bts', rel, wib.astype(jnp.float32)) * idx_scale
        score = jnp.where(adm[None], score, -jnp.inf)
        _, sel = lax.top_k(score, topk)
        valid = key_chunk[sel] <= q_chunk[None, :, None]
        ks = gather(k, sel)
        vs = gather(v, sel)
        s = jnp.einsum('bthd,btkhd->bthk', qb, ks).astype(jnp.float32) * (Dh ** -0.5)
        s = jnp.where(valid[:, :, None, :], s, -jnp.inf)
        p = jax.nn.softmax(s, axis=-1).astype(v.dtype)
        return jnp.einsum('bthk,btkhd->bthd', p, vs)

    out = lax.map(block, jnp.arange(n_blocks))
    return out.transpose(1, 0, 2, 3, 4).reshape(B, S, H * Dh)

def memory_cross_attention(h, mem, g_mem, w_q, w_kv, q_norm, k_norm, w_o):
    B, S, _ = h.shape
    M = mem.shape[1]
    m = rmsnorm(mem, g_mem)
    q = (h @ w_q).reshape(B, S, MEM_HEADS, MEM_HEAD_DIM)
    kv = (m @ w_kv).reshape(B, M, 2, MEM_HEADS, MEM_HEAD_DIM)
    q = rmsnorm(q, q_norm)
    k = rmsnorm(kv[:, :, 0], k_norm)
    v = kv[:, :, 1]
    s = jnp.einsum('bshd,bmhd->bhsm', q, k).astype(jnp.float32) * (MEM_HEAD_DIM ** -0.5)
    p = jax.nn.softmax(s, axis=-1).astype(v.dtype)
    o = jnp.einsum('bhsm,bmhd->bshd', p, v).reshape(B, S, MEM_WIDTH)
    return o @ w_o

def hierarchical_moe(h, wg_router, bg_router, we_router, be_router, w_gate, w_up, w_down):
    B, S, D = h.shape
    hf = h.reshape(B * S, D)
    g_logits = (hf @ wg_router + bg_router).astype(jnp.float32)
    g_prob = jax.nn.softmax(g_logits, axis=-1)
    g_sel = jnp.argmax(g_logits, axis=-1)
    g_w = jnp.take_along_axis(g_prob, g_sel[:, None], axis=1)
    e_logits = (hf @ we_router + be_router).astype(jnp.float32)
    e_logits = e_logits.reshape(-1, N_GROUPS, EXPERTS_PER_GROUP)
    e_in = jnp.take_along_axis(e_logits, g_sel[:, None, None], axis=1)[:, 0]
    top_v, top_i = lax.top_k(e_in, TOP_K_EXPERTS)
    top_w = jax.nn.softmax(top_v, axis=-1) * g_w
    exp_w = jnp.sum(jax.nn.one_hot(top_i, EXPERTS_PER_GROUP, dtype=jnp.float32)
                    * top_w[..., None], axis=1)
    gates = jax.nn.one_hot(g_sel, N_GROUPS, dtype=jnp.float32)[:, :, None] * exp_w[:, None, :]
    out = jnp.zeros_like(hf)
    for g in range(N_GROUPS):
        a = jnp.einsum('nd,edf->nef', hf, w_gate[g])
        b = jnp.einsum('nd,edf->nef', hf, w_up[g])
        hid = jax.nn.silu(a) * b * gates[:, g, :, None].astype(hf.dtype)
        out = out + jnp.einsum('nef,efd->nd', hid, w_down[g])
    return out.reshape(B, S, D)

def first_inputs(seed: int = 0) -> dict:
    key = jax.random.key(seed)
    ks = jax.random.split(key, 32)
    f32 = jnp.float32
    L = DEPTH

    def nrm(k, shape, scale):
        return jax.random.normal(k, shape, f32) * scale

    def gain(k, shape):
        return 1.0 + 0.02 * jax.random.normal(k, shape, f32)

    return {
        "x": nrm(ks[0], (BATCH, SEQ, D_MODEL), 1.0),
        "mem": nrm(ks[1], (BATCH, MEM_TOKENS, D_MODEL), 1.0),
        "mix_norm": gain(ks[2], (L, D_MODEL)),
        "w_in": nrm(ks[3], (L, D_MODEL, IN_COLS), D_MODEL ** -0.5),
        "pool_w": nrm(ks[4], (L, len(POOL_WINDOWS), POOL_GROUP, POOL_GROUP), POOL_GROUP ** -0.5),
        "pool_scale": gain(ks[5], (L, POOL_WIDTH)),
        "q_norm": gain(ks[6], (L, HEAD_DIM)),
        "k_norm": gain(ks[7], (L, HEAD_DIM)),
        "idx_k_norm": gain(ks[8], (L, IDX_DIM)),
        "w_out": nrm(ks[9], (L, MIX_WIDTH, D_MODEL), MIX_WIDTH ** -0.5),
        "xattn_norm": gain(ks[10], (L, D_MODEL)),
        "mem_norm": gain(ks[11], (L, D_MODEL)),
        "xattn_wq": nrm(ks[12], (L, D_MODEL, MEM_WIDTH), D_MODEL ** -0.5),
        "xattn_wkv": nrm(ks[13], (L, D_MODEL, 2 * MEM_WIDTH), D_MODEL ** -0.5),
        "xattn_q_norm": gain(ks[14], (L, MEM_HEAD_DIM)),
        "xattn_k_norm": gain(ks[15], (L, MEM_HEAD_DIM)),
        "xattn_wo": nrm(ks[16], (L, MEM_WIDTH, D_MODEL), MEM_WIDTH ** -0.5),
        "ffn_norm": gain(ks[17], (L, D_MODEL)),
        "router_group_w": nrm(ks[18], (L, D_MODEL, N_GROUPS), D_MODEL ** -0.5),
        "router_group_b": nrm(ks[19], (L, N_GROUPS), 0.01),
        "router_expert_w": nrm(ks[20], (L, D_MODEL, N_GROUPS * EXPERTS_PER_GROUP), D_MODEL ** -0.5),
        "router_expert_b": nrm(ks[21], (L, N_GROUPS * EXPERTS_PER_GROUP), 0.01),
        "expert_w_gate": nrm(ks[22], (L, N_GROUPS, EXPERTS_PER_GROUP, D_MODEL, EXPERT_FF), D_MODEL ** -0.5),
        "expert_w_up": nrm(ks[23], (L, N_GROUPS, EXPERTS_PER_GROUP, D_MODEL, EXPERT_FF), D_MODEL ** -0.5),
        "expert_w_down": nrm(ks[24], (L, N_GROUPS, EXPERTS_PER_GROUP, EXPERT_FF, D_MODEL), EXPERT_FF ** -0.5),
    }

def first_block(x, mem, mix_norm, w_in, pool_w, pool_scale, q_norm, k_norm, idx_k_norm, w_out,
              xattn_norm, mem_norm, xattn_wq, xattn_wkv, xattn_q_norm, xattn_k_norm, xattn_wo,
              ffn_norm, router_group_w, router_group_b, router_expert_w, router_expert_b,
              expert_w_gate, expert_w_up, expert_w_down):
    B, S, _ = x.shape
    cos_a, sin_a = rope_tables(S, HEAD_DIM)
    cos_i, sin_i = rope_tables(S, IDX_DIM)
    for l in range(DEPTH):
        h = rmsnorm(x, mix_norm[l])
        z = h @ w_in[l]
        u = z[..., OFF_POOL:OFF_Q]
        q = z[..., OFF_Q:OFF_K].reshape(B, S, ATTN_HEADS, HEAD_DIM)
        k = z[..., OFF_K:OFF_V].reshape(B, S, ATTN_HEADS, HEAD_DIM)
        v = z[..., OFF_V:OFF_QI].reshape(B, S, ATTN_HEADS, HEAD_DIM)
        qi = z[..., OFF_QI:OFF_KI].reshape(B, S, IDX_HEADS, IDX_DIM)
        ki = z[..., OFF_KI:OFF_WI]
        wi = z[..., OFF_WI:IN_COLS]
        q = apply_rope(rmsnorm(q, q_norm[l]), cos_a, sin_a)
        k = apply_rope(rmsnorm(k, k_norm[l]), cos_a, sin_a)
        qi = apply_rope(qi, cos_i, sin_i)
        ki = apply_rope(rmsnorm(ki, idx_k_norm[l])[:, :, None, :], cos_i, sin_i)[:, :, 0]
        y_pool = pool_mixer(u, pool_w[l], pool_scale[l])
        y_attn = dsa_attention(q, k, v, qi, ki, wi)
        x = x + jnp.concatenate([y_pool, y_attn], axis=-1) @ w_out[l]
        h = rmsnorm(x, xattn_norm[l])
        x = x + memory_cross_attention(h, mem, mem_norm[l], xattn_wq[l], xattn_wkv[l],
                                       xattn_q_norm[l], xattn_k_norm[l], xattn_wo[l])
        h = rmsnorm(x, ffn_norm[l])
        x = x + hierarchical_moe(h, router_group_w[l], router_group_b[l], router_expert_w[l],
                                 router_expert_b[l], expert_w_gate[l], expert_w_up[l],
                                 expert_w_down[l])
    return x


GRID_W = 64
NA_HEADS = 8
NA_HEAD_DIM = 64
NA_WIN_ROWS_MAX = 8
NA_WIN_COLS = 16
NA_WIDTH = NA_HEADS * NA_HEAD_DIM
MLA_HEADS = 8
MLA_Q_RANK = 256
MLA_KV_RANK = 128
MLA_NOPE_DIM = 64
MLA_ROPE_DIM = 32
MLA_V_DIM = 64
MLA_QK_DIM = MLA_NOPE_DIM + MLA_ROPE_DIM
MLA_WIDTH = MLA_HEADS * MLA_V_DIM
ATTN_BLOCK = 128
IN_SPLITS = (NA_WIDTH, NA_WIDTH, NA_WIDTH, MLA_Q_RANK, MLA_KV_RANK, MLA_ROPE_DIM, D_MODEL, D_MODEL)
IN_COLS_2 = 3 * NA_WIDTH + MLA_Q_RANK + MLA_KV_RANK + MLA_ROPE_DIM + 2 * D_MODEL
N_EXPERTS = 64
TOP_K = 8
N_GROUPS_2 = 8
TOPK_GROUPS = 4
SHARED_FF = 256
ROUTED_SCALE = 2.5
MOE_CHUNK = 128
NEG_BIG = -1e30


def rms_norm(x, g):
    xf = x.astype(jnp.float32)
    y = xf * lax.rsqrt(jnp.mean(xf * xf, axis=-1, keepdims=True) + EPS)
    return (y * g.astype(jnp.float32)).astype(x.dtype)

def apply_rope_2(x, positions):
    half = x.shape[-1] // 2
    inv_freq = ROPE_THETA ** (-jnp.arange(half, dtype=jnp.float32) / half)
    ang = positions.astype(jnp.float32)[:, :, None, None] * inv_freq
    cos, sin = jnp.cos(ang), jnp.sin(ang)
    xf = x.astype(jnp.float32)
    x1, x2 = xf[..., :half], xf[..., half:]
    return jnp.concatenate([x1 * cos - x2 * sin, x2 * cos + x1 * sin], axis=-1).astype(x.dtype)

def neighbourhood_attention(q, k, v, rpb):
    B, S, H, Dh = q.shape
    R = S // GRID_W
    kh = min(NA_WIN_ROWS_MAX, R)
    to_grid = lambda t: t.reshape(B, R, GRID_W, H, Dh).transpose(0, 3, 1, 2, 4)
    qg, kg, vg = to_grid(q), to_grid(k), to_grid(v)
    rows = jnp.arange(R)
    row_start = jnp.clip(rows - kh // 2, 0, R - kh)
    key_rows = row_start[:, None] + jnp.arange(kh)[None, :]
    kb = kg[:, :, key_rows]
    vb = vg[:, :, key_rows]
    s = jnp.einsum('bhrqd,bhrjkd->bhrqjk', qg, kb).astype(jnp.float32) * (Dh ** -0.5)
    cols = jnp.arange(GRID_W)
    col_start = jnp.clip(cols - NA_WIN_COLS // 2, 0, GRID_W - NA_WIN_COLS)
    in_win = (cols[None, :] >= col_start[:, None]) & (cols[None, :] < col_start[:, None] + NA_WIN_COLS)
    dr = key_rows - rows[:, None]
    dc = jnp.clip(cols[None, :] - cols[:, None], -(NA_WIN_COLS - 1), NA_WIN_COLS - 1)
    bias = rpb[:, dr[:, None, :, None] + (NA_WIN_ROWS_MAX - 1),
               dc[None, :, None, :] + (NA_WIN_COLS - 1)]
    s = s + bias.astype(jnp.float32)[None]
    s = jnp.where(in_win[:, None, :], s, NEG_BIG)
    p = jax.nn.softmax(s.reshape(B, H, R, GRID_W, kh * GRID_W), axis=-1)
    p = p.reshape(B, H, R, GRID_W, kh, GRID_W).astype(v.dtype)
    o = jnp.einsum('bhrqjk,bhrjkd->bhrqd', p, vb)
    return o.transpose(0, 2, 3, 1, 4).reshape(B, S, H * Dh)

def blocked_full_attention(q, k, v):
    B, S, H, Dqk = q.shape
    Dv = v.shape[-1]
    nb = S // ATTN_BLOCK
    qb = q.reshape(B, nb, ATTN_BLOCK, H, Dqk).transpose(1, 0, 2, 3, 4)
    scale = Dqk ** -0.5

    def one_block(q_blk):
        s = jnp.einsum('bqhd,bkhd->bhqk', q_blk, k).astype(jnp.float32) * scale
        p = jax.nn.softmax(s, axis=-1).astype(v.dtype)
        return jnp.einsum('bhqk,bkhd->bqhd', p, v)

    o = lax.map(one_block, qb)
    return o.transpose(1, 0, 2, 3, 4).reshape(B, S, H * Dv)

def moe_ffn(h, w_router, e_bias, w_eg, w_eu, w_ed, w_sg, w_su, w_sd):
    B, S, D = h.shape
    t = h.reshape(-1, D)
    T = t.shape[0]
    scores = jax.nn.sigmoid((t @ w_router).astype(jnp.float32))
    sel = scores + e_bias.astype(jnp.float32)
    grp = sel.reshape(T, N_GROUPS_2, N_EXPERTS // N_GROUPS_2)
    grp_score = jnp.sum(lax.top_k(grp, 2)[0], axis=-1)
    _, gidx = lax.top_k(grp_score, TOPK_GROUPS)
    gmask = jnp.sum(jax.nn.one_hot(gidx, N_GROUPS_2, dtype=jnp.float32), axis=-2)
    emask = jnp.repeat(gmask, N_EXPERTS // N_GROUPS_2, axis=-1)
    sel = jnp.where(emask > 0, sel, -jnp.inf)
    _, eidx = lax.top_k(sel, TOP_K)
    w = jnp.take_along_axis(scores, eidx, axis=-1)
    w = w / jnp.sum(w, axis=-1, keepdims=True) * ROUTED_SCALE
    gates = jnp.sum(jax.nn.one_hot(eidx, N_EXPERTS, dtype=jnp.float32) * w[..., None], axis=-2)
    tc = t.reshape(-1, MOE_CHUNK, D)
    gc = gates.reshape(-1, MOE_CHUNK, N_EXPERTS).astype(t.dtype)

    def expert_chunk(args):
        xc, gch = args
        hg = jnp.einsum('cd,edf->cef', xc, w_eg)
        hu = jnp.einsum('cd,edf->cef', xc, w_eu)
        a = jax.nn.silu(hg) * hu * gch[..., None]
        return jnp.einsum('cef,efd->cd', a, w_ed)

    routed = lax.map(expert_chunk, (tc, gc)).reshape(T, D)
    shared = (jax.nn.silu(t @ w_sg) * (t @ w_su)) @ w_sd
    return (routed + shared).reshape(B, S, D)

def second_inputs(seed: int = 0) -> dict:
    key = jax.random.key(seed)
    ks = iter(jax.random.split(key, 32))
    f32 = jnp.float32
    nrm = lambda shape, s: jax.random.normal(next(ks), shape, f32) * s
    gain = lambda shape: 1.0 + 0.05 * jax.random.normal(next(ks), shape, f32)
    L, D, E, F = DEPTH, D_MODEL, N_EXPERTS, EXPERT_FF
    x = jax.random.normal(next(ks), (BATCH, SEQ, D), f32)
    c = jax.random.normal(next(ks), (BATCH, D), f32)
    positions = jnp.broadcast_to(jnp.arange(SEQ, dtype=jnp.int32)[None, :], (BATCH, SEQ))
    return {
        "x": x,
        "c": c,
        "positions": positions,
        "w_ada": nrm((L, D, 6 * D), 0.3 * D ** -0.5),
        "b_ada": nrm((L, 6 * D), 0.02),
        "g_norm1": gain((L, D)),
        "w_in": nrm((L, D, IN_COLS_2), D ** -0.5),
        "g_na_q": gain((L, NA_HEAD_DIM)),
        "g_na_k": gain((L, NA_HEAD_DIM)),
        "na_rpb": nrm((L, NA_HEADS, 2 * NA_WIN_ROWS_MAX - 1, 2 * NA_WIN_COLS - 1), 0.1),
        "g_q_lat": gain((L, MLA_Q_RANK)),
        "w_uq": nrm((L, MLA_Q_RANK, MLA_HEADS * MLA_QK_DIM), MLA_Q_RANK ** -0.5),
        "g_kv_lat": gain((L, MLA_KV_RANK)),
        "w_ukv": nrm((L, MLA_KV_RANK, MLA_HEADS * (MLA_NOPE_DIM + MLA_V_DIM)), MLA_KV_RANK ** -0.5),
        "g_mla_q": gain((L, MLA_QK_DIM)),
        "g_mla_k": gain((L, MLA_QK_DIM)),
        "w_proj_na": nrm((L, NA_WIDTH, D), NA_WIDTH ** -0.5),
        "w_proj_mla": nrm((L, MLA_WIDTH, D), MLA_WIDTH ** -0.5),
        "w_out": nrm((L, D, D), D ** -0.5),
        "g_norm2": gain((L, D)),
        "w_router": nrm((L, D, E), D ** -0.5),
        "e_bias": nrm((L, E), 0.01),
        "w_exp_gate": nrm((L, E, D, F), D ** -0.5),
        "w_exp_up": nrm((L, E, D, F), D ** -0.5),
        "w_exp_down": nrm((L, E, F, D), F ** -0.5),
        "w_sh_gate": nrm((L, D, SHARED_FF), D ** -0.5),
        "w_sh_up": nrm((L, D, SHARED_FF), D ** -0.5),
        "w_sh_down": nrm((L, SHARED_FF, D), SHARED_FF ** -0.5),
    }

def second_block(x, c, positions, w_ada, b_ada, g_norm1, w_in, g_na_q, g_na_k, na_rpb,
              g_q_lat, w_uq, g_kv_lat, w_ukv, g_mla_q, g_mla_k, w_proj_na, w_proj_mla,
              w_out, g_norm2, w_router, e_bias, w_exp_gate, w_exp_up, w_exp_down,
              w_sh_gate, w_sh_up, w_sh_down):
    B, S, D = x.shape
    split_at = list(np.cumsum(IN_SPLITS)[:-1])
    for l in range(DEPTH):
        mod = jax.nn.silu(c) @ w_ada[l] + b_ada[l]
        shift1, scale1, gate1, shift2, scale2, gate2 = jnp.split(mod[:, None, :], 6, axis=-1)

        h = rms_norm(x, g_norm1[l]) * (1.0 + scale1) + shift1
        proj = h @ w_in[l]
        na_q, na_k, na_v, q_lat, kv_lat, k_rot, gate_na, gate_mla = jnp.split(proj, split_at, axis=-1)

        qa = rms_norm(na_q.reshape(B, S, NA_HEADS, NA_HEAD_DIM), g_na_q[l])
        ka = rms_norm(na_k.reshape(B, S, NA_HEADS, NA_HEAD_DIM), g_na_k[l])
        va = na_v.reshape(B, S, NA_HEADS, NA_HEAD_DIM)
        y_na = neighbourhood_attention(qa, ka, va, na_rpb[l])

        qm = (rms_norm(q_lat, g_q_lat[l]) @ w_uq[l]).reshape(B, S, MLA_HEADS, MLA_QK_DIM)
        q_nope, q_rope = qm[..., :MLA_NOPE_DIM], apply_rope_2(qm[..., MLA_NOPE_DIM:], positions)
        kvm = (rms_norm(kv_lat, g_kv_lat[l]) @ w_ukv[l]).reshape(B, S, MLA_HEADS, MLA_NOPE_DIM + MLA_V_DIM)
        k_nope, vm = kvm[..., :MLA_NOPE_DIM], kvm[..., MLA_NOPE_DIM:]
        k_rope = jnp.broadcast_to(apply_rope_2(k_rot[:, :, None, :], positions), (B, S, MLA_HEADS, MLA_ROPE_DIM))
        qm = rms_norm(jnp.concatenate([q_nope, q_rope], axis=-1), g_mla_q[l])
        km = rms_norm(jnp.concatenate([k_nope, k_rope], axis=-1), g_mla_k[l])
        y_mla = blocked_full_attention(qm, km, vm)

        merged = (jax.nn.sigmoid(gate_na) * (y_na @ w_proj_na[l])
                  + jax.nn.sigmoid(gate_mla) * (y_mla @ w_proj_mla[l]))
        x = x + gate1 * (merged @ w_out[l])

        h2 = rms_norm(x, g_norm2[l]) * (1.0 + scale2) + shift2
        y_ffn = moe_ffn(h2, w_router[l], e_bias[l], w_exp_gate[l], w_exp_up[l], w_exp_down[l],
                        w_sh_gate[l], w_sh_up[l], w_sh_down[l])
        x = x + gate2 * y_ffn
    return x


def setup_inputs(seed=0):
    out = dict(first_inputs(seed))
    for name, value in second_inputs(seed + 1).items():
        if name != "x":
            out[name + "_2"] = value
    return out


def reference(
    x, mem, mix_norm, w_in, pool_w, pool_scale, q_norm, k_norm, idx_k_norm, w_out, xattn_norm,
    mem_norm, xattn_wq, xattn_wkv, xattn_q_norm, xattn_k_norm, xattn_wo, ffn_norm,
    router_group_w, router_group_b, router_expert_w, router_expert_b, expert_w_gate,
    expert_w_up, expert_w_down, c_2, positions_2, w_ada_2, b_ada_2, g_norm1_2, w_in_2, g_na_q_2,
    g_na_k_2, na_rpb_2, g_q_lat_2, w_uq_2, g_kv_lat_2, w_ukv_2, g_mla_q_2, g_mla_k_2,
    w_proj_na_2, w_proj_mla_2, w_out_2, g_norm2_2, w_router_2, e_bias_2, w_exp_gate_2,
    w_exp_up_2, w_exp_down_2, w_sh_gate_2, w_sh_up_2, w_sh_down_2,
):
    x = first_block(
        x, mem, mix_norm, w_in, pool_w, pool_scale, q_norm, k_norm, idx_k_norm, w_out,
        xattn_norm, mem_norm, xattn_wq, xattn_wkv, xattn_q_norm, xattn_k_norm, xattn_wo,
        ffn_norm, router_group_w, router_group_b, router_expert_w, router_expert_b,
        expert_w_gate, expert_w_up, expert_w_down,
    )
    return second_block(
        x, c_2, positions_2, w_ada_2, b_ada_2, g_norm1_2, w_in_2, g_na_q_2, g_na_k_2, na_rpb_2,
        g_q_lat_2, w_uq_2, g_kv_lat_2, w_ukv_2, g_mla_q_2, g_mla_k_2, w_proj_na_2, w_proj_mla_2,
        w_out_2, g_norm2_2, w_router_2, e_bias_2, w_exp_gate_2, w_exp_up_2, w_exp_down_2,
        w_sh_gate_2, w_sh_up_2, w_sh_down_2,
    )


_drawn_inputs = setup_inputs


def setup_inputs(seed=0):
    import zlib

    import numpy as np

    out = dict(_drawn_inputs(seed))
    spreads = {}
    factors = {'q_norm': 8.0,
     'k_norm': 3.815,
     'xattn_norm': 6.514,
     'mem_norm': 8.0,
     'xattn_q_norm': 8.0,
     'xattn_k_norm': 4.551,
     'router_group_b': 40.747,
     'router_expert_b': 27.76,
     'g_norm1_2': 8.0,
     'g_na_q_2': 8.0,
     'g_na_k_2': 8.0,
     'na_rpb_2': 44.965,
     'g_q_lat_2': 8.0,
     'w_uq_2': 4.668,
     'g_kv_lat_2': 8.0,
     'g_mla_q_2': 8.0,
     'g_mla_k_2': 8.0,
     'ffn_norm': 7.555,
     'g_norm2_2': 8.0,
     'w_router_2': 4.473,
     'e_bias_2': 8.0,
     'w_exp_gate_2': 4.5,
     'w_exp_up_2': 4.215,
     'w_exp_down_2': 4.182,
     'w_sh_gate_2': 3.987,
     'w_sh_up_2': 3.697,
     'w_sh_down_2': 3.718}
    for name, (base, spread) in spreads.items():
        noise = np.random.default_rng([zlib.crc32(name.encode()), seed]).standard_normal(out[name].shape)
        drawn = base * np.exp(spread * noise) if base else spread * noise
        out[name] = __import__('jax').numpy.asarray(drawn.astype(out[name].dtype))
    for name, factor in factors.items():
        out[name] = (out[name] * factor).astype(out[name].dtype)
    return out
```

```python
from contextlib import ExitStack

import numpy as np

import concourse.bass as bass
from concourse import mybir

F32 = mybir.dt.float32
I32 = mybir.dt.int32
U32 = mybir.dt.uint32
ALU = mybir.AluOpType
ACT = mybir.ActivationFunctionType
X = mybir.AxisListType.X

P = 128
D = 1024
KD = D // P
S = 256
TT = S // P
EPS = 1e-6
HEADS = 8
HD = 64
XH = 4
XD = 128
E1, G1, EPG1 = 32, 4, 8
E2, G2, EPG2 = 64, 8, 8
FF = 256
TOPK_KEYS = 64
QK = 96
ROPE_HALF = 16
BIG = 1e30
FLT = 3.0e38
U0, Q0, K0, V0, QI0, KI0, WI0, Z1 = 0, 512, 1024, 1536, 2048, 2560, 2624, 2632
NQ0, NK0, NV0, QL0, KL0, KR0, GN0, GM0, Z2 = 0, 512, 1024, 1536, 1792, 1920, 1952, 2976, 4000
ADA = 6 * D
ADA_STEP = D
ADA_BUFFERS = 2
ADA_DVE = 2
TWO_PI = 2 * np.pi
TAKES = {1: 2, 2: 8}
ROWS_OF = {1: 64, 2: 128}
EXPERTS = {1: E1, 2: E2}
ITEMS = {n: 2 * ((EXPERTS[n] + (S * TAKES[n] - EXPERTS[n]) // ROWS_OF[n] + 1) // 2) + 2 for n in TAKES}
RPB = 8 * 15 * 31

COLS = [("mix_norm", 8), ("xattn_norm", 8), ("mem_norm", 8), ("ffn_norm", 8), ("g_norm1_2", 8),
        ("g_norm2_2", 8), ("pool_scale", 4), ("c_2", 8)]
COL, _n = {}, 0
for _name, _rows in COLS:
    COL[_name] = _n
    _n += _rows
N_COLS = _n
ROWS = [("q_norm", 64), ("k_norm", 64), ("idx_k_norm", 64), ("xattn_q_norm", 128),
        ("xattn_k_norm", 128), ("g_na_q_2", 64), ("g_na_k_2", 64), ("g_q_lat_2", 256),
        ("g_kv_lat_2", 128), ("g_mla_q_2", 96), ("g_mla_k_2", 96), ("router_group_b", 4),
        ("router_expert_b", 32), ("e_bias_2", 64)]
ROW, ROW_W = {}, 0
for _name, _w in ROWS:
    ROW[_name] = (ROW_W, _w)
    ROW_W += _w


X_NORMS = ["x1", "x2", "x3", "x4", "x5"]
NORMS = ["x1", "mem", "front", "km", "x2", "qm", "x3", "x4", "nqk", "mq", "mk", "x5"]


def shape_constants():
    f = np.float32
    inv = (f(10000.0) ** (-np.arange(0, HD, 2, dtype=f) / f(HD))).astype(f)
    ang = (np.arange(S, dtype=f)[:, None] * inv[None, :]).astype(f).astype(np.float64)
    cos, sin = np.cos(ang), np.sin(ang)
    rope = np.concatenate([cos, cos, -sin, sin], axis=1).astype(f)
    pool = np.zeros((4, S, S), f)
    for g, w in enumerate((2, 4, 8, 16)):
        for t in range(S):
            n = min(t + 1, w)
            pool[g, t - n + 1:t + 1, t] = f(1.0) / f(n)
            pool[g, t, t] -= f(1.0)
    chunk = np.arange(S) // 64
    admissible = np.where(chunk[None, :] <= chunk[:, None], 0.0, -BIG).astype(f)
    col = np.arange(64)
    start = np.clip(col - 8, 0, 48)
    inside = (col[None, :] >= start[:, None]) & (col[None, :] < start[:, None] + 16)
    window = np.where(inside, 0.0, -BIG).astype(f)
    window = np.concatenate([window, window], axis=0)
    earlier = (np.arange(8)[None, :] < np.arange(8)[:, None]).astype(f).reshape(1, 64)
    inv2 = (f(10000.0) ** (-np.arange(ROPE_HALF, dtype=f) / f(ROPE_HALF))).astype(f).reshape(1, 16)
    i = np.arange(P)
    lists = np.zeros((P, 2 * P + 2 + E2 + 1), f)
    lists[:, 0:P] = i[:, None] < i[None, :]
    lists[:, P:2 * P] = i[None, :]
    lists[:, 2 * P] = i
    lists[:, 2 * P + 1] = i + P
    lists[:, 2 * P + 2:] = i[:, None] < np.arange(E2 + 1)[None, :]
    return dict(c_lists=lists, c_rope=rope, c_pool=pool, c_admissible=admissible, c_window=window,
                c_earlier=earlier, c_inv2=inv2)


def plan_groups():
    A, V = "act", "dve"
    one = [("cols", V)]
    one += [(f"xT1.{i}", V) for i in range(4)]
    one += [(f"z.{c}.{t}", A) for c in range(4) for t in range(2)]
    one += [(f"memT.{i}", V) for i in range(4)]
    one += [(f"z.{c}.{t}", A) for c in (4, 5) for t in range(2)]
    one += [("kiT", A), ("qiT.0", A), ("qiT.1", A)]
    one += [(f"idx.{i}", A) for i in range(6)]
    one += [(f"kv.{c}.{t}", A) for c in range(2) for t in range(2)]
    one += [("mixT.0", A), ("mixT.1", A), ("ypT.0", V), ("ypT.1", V)]
    one += [(f"{a}T.{t}", A) for a in "qk" for t in range(2)]
    one += [("kmT.0", A), ("kmT.1", A)]

    def attend(name, scores, turns):
        out = []
        for t in range(2):
            out += [(f"{name}.s.{t}.{i}", V) for i in range(scores[t])]
        for t in range(2):
            out += [(f"{name}.p.{t}.{i}", A) for i in range(turns[t])]
            out += [(f"{name}.o.{t}", V)]
        return out + [(f"{name}.yT.{t}", A) for t in range(2)]

    one += attend("dsa", (2, 4), (2, 4))
    one += [(f"wout.{n}.{t}", V) for n in range(2) for t in range(2)]
    one += [(f"xT2.{i}", V) for i in range(4)]
    one += [("wq.0", A), ("wq.1", A), ("qmT.0", A), ("qmT.1", A)]
    one += attend("mem", (2, 2), (2, 2))
    one += [(f"wo.{n}.{t}", V) for n in range(2) for t in range(2)]
    one += [(f"xT3.{i}", V) for i in range(4)]
    one += [("route1.0", V), ("route1.1", V), ("rank1", V), ("start1", V), ("items1", V), ("mod", A)]
    one += [("tokens1", V)] + [(f"gate.{i}", A) for i in range(4)]
    two = [(f"xT4.{i}", V) for i in range(4)]
    two += [(f"y.{c}.{t}", A) for c in range(8) for t in range(2)]
    two += [(f"n{a}T.{t}", A) for a in "qk" for t in range(2)]
    two += attend("na", (4, 4), (4, 4))
    two += [("qlT.0", A), ("qlT.1", A), ("klT", A)]
    two += [(f"uq.{c}.{t}", A) for t in range(2) for c in range(2)]
    two += [(f"ukv.{c}.{t}", A) for t in range(2) for c in range(2)]
    two += [(f"pna.{n}.{t}", V) for n in range(2) for t in range(2)]
    two += [(f"m{a}T.{t}.{i}", A) for a in "qk" for t in range(2) for i in range(2)]
    two += attend("mla", (4, 4), (4, 4))
    two += [(f"pmla.{n}.{t}", V) for n in range(2) for t in range(2)]
    two += [(f"mgT.{i}", A) for i in range(4)]
    two += [(f"wout2.{n}.{t}", V) for n in range(2) for t in range(2)]
    two += [(f"xT5.{i}", V) for i in range(4)]
    two += [("route2.0", V), ("route2.1", V), ("shgu.0", V), ("shgu.1", V), ("shT.0", A), ("shT.1", A)]
    two += [(f"shdown.{n}.{t}", A) for n in range(2) for t in range(2)]
    two += [("rank2", V), ("start2", V), ("items2", V), ("tokens2", V)]
    return [one, two]


def plan_jobs():
    one = [("z.0", "w_in", QI0, 512, 8), ("z.1", "w_in", KI0, 72, 8), ("z.2", "w_in", Q0, 512, 8),
           ("z.3", "w_in", K0, 512, 8), ("z.4", "w_in", V0, 512, 8), ("z.5", "w_in", U0, 512, 8),
           ("kv.0", "xattn_wkv", 0, 512, 8), ("kv.1", "xattn_wkv", 512, 512, 8),
           ("wout.0", "w_out", 0, 512, 8), ("wout.1", "w_out", 512, 512, 8),
           ("wq", "xattn_wq", 0, 512, 8), ("wo", "xattn_wo", 0, 1024, 4)]
    two = [(f"y.{c}", "w_in_2", a, n, 8) for c, (a, n) in enumerate(Y_CHUNKS)]
    two += [("uq", "w_uq_2", 0, 768, 2), ("ukv", "w_ukv_2", 0, 1024, 1),
            ("pna", "w_proj_na_2", 0, 1024, 4), ("pmla", "w_proj_mla_2", 0, 1024, 4),
            ("wout2.0", "w_out_2", 0, 512, 8), ("wout2.1", "w_out_2", 512, 512, 8),
            ("route2", "w_router_2", 0, E2, 8), ("shgu", "w_sh_up_2", 0, 2 * FF, 8),
            ("shdown", "w_sh_down_2", 0, D, 2)]
    return [one, two]


Y_CHUNKS = [(NQ0, 512), (NK0, 512), (NV0, 512), (QL0, 416), (GN0, 512), (GN0 + 512, 512),
            (GM0, 512), (GM0 + 512, 512)]
Z_CHUNKS = [(QI0, 512), (KI0, 72), (Q0, 512), (K0, 512), (V0, 512), (U0, 512)]
SLOTS = 3


def build_program(nc, A, out, dbg=None):
    groups, jobs = plan_groups(), plan_jobs()
    group_at, reads_before = {}, {}
    for seg, listed in enumerate(groups):
        seen = {"act": sum(r == "act" for g in groups[:seg] for _, r in g),
                "dve": sum(r == "dve" for g in groups[:seg] for _, r in g)}
        base = sum(len(g) for g in groups[:seg])
        for n, (key, reader) in enumerate(listed):
            seen[reader] += 1
            group_at[key] = (seg, n, base + n + 1, reader, seen[reader])
    job_at = {}
    for seg, listed in enumerate(jobs):
        base = sum(len(g) for g in jobs[:seg])
        for n, job in enumerate(listed):
            job_at[job[0]] = (seg, base + n, job)
    n_jobs_one = len(jobs[0])

    ctx = ExitStack()
    with ctx:
        def sb(name, shape, dt=F32):
            return ctx.enter_context(nc.sbuf_tensor(name, shape, dt))[:]

        sems = {}

        def E(name):
            if name not in sems:
                sems[name] = ctx.enter_context(nc.semaphore(name))
            return sems[name]

        ring = sb("ring", [P, 6, 2048])
        x = sb("x", [P, 2, D])
        hT = sb("hT", [P, 8, S])
        Z = sb("Z", [P, 2, Z2])
        qT = sb("qT", [P, 8, S])
        kT = sb("kT", [P, 8, S])
        qiT = sb("qiT", [P, 4, S])
        kiT = sb("kiT", [P, S])
        PR = sb("PR", [P, 2, HEADS, S])
        PT = sb("PT", [P, 16, P])
        yn = sb("yn", [P, 2, 512])
        yT = sb("yT", [P, 8, S])
        kmT_vm = sb("kmT_vm", [P, 8, S])
        bias = sb("bias", [P, 2, HEADS, S])
        gateB = sb("gateB", [P, 2, D])
        tmp = sb("tmp", [P, 2, D])
        ident = sb("ident", [P, P])
        ones = sb("ones", [P, P])
        cols = sb("cols", [P, P])
        rows = sb("rows", [P, ROW_W])
        rope = sb("rope", [P, 2, 128])
        window = sb("window", [P, 64])
        earlier = sb("earlier", [P, 64])
        inv2 = sb("inv2", [P, 16])
        pos_i = sb("pos_i", [P, 2], I32)
        pos_f = sb("pos_f", [P, 2])
        trig = sb("trig", [P, 4, 2, 16])
        st = sb("st", [P, 512])
        gates = sb("gates", [P, 2, E2 + 2])
        rw1 = sb("rw1", [P, 8, 36])
        silc = sb("silc", [P, 8])
        modc = sb("modc", [P, 32])
        gs4 = sb("gs4", [P, 16])
        eps = sb("eps", [P, 1])
        lists = sb("lists", [P, 2 * P + 2 + E2 + 1])
        token_list = sb("token_list", [P, max(ITEMS.values())], U32)
        token_now = sb("token_now", [P, 2], U32)
        y_rows = sb("y_rows", [P, 2, 8], U32)
        share = sb("share", [P, 2, 8])
        item_expert = sb("item_expert", [1, P], I32)
        item_base = sb("item_base", [1, P + 1], I32)
        pairs_n = sb("pairs_n", [1, 1], I32)

        bank = ctx.enter_context(nc.psum_tensor("bank", [P, 8, 512], F32))[:]

        rpb_copies = nc.dram_tensor("rpb_copies", (64, RPB + 1), F32, kind="Internal").ap()

        xn_dram = {n: nc.dram_tensor(f"xn_dram{n}", (S, D), F32, kind="Internal").ap() for n in TAKES}
        y_dram = {n: nc.dram_tensor(f"y_dram{n}", (S * TAKES[n] + ROWS_OF[n], D), F32, kind="Internal").ap() for n in TAKES}

        adm = yT[:, 0:2, :]
        rowsC = yn.rearrange("p t n -> p (t n)")[:, 0:P]
        tri, iota, tok_id, order = lists[:, 0:P], lists[:, P:2 * P], lists[:, 2 * P:2 * P + 2], lists[:, 2 * P + 2:]
        kmT = kmT_vm[:, 0:4, :]
        vm = kmT_vm[:, 4:8, :].rearrange("p a s -> p (a s)").rearrange("p (t n) -> p t n", t=2)
        PRf = PR[:].rearrange("p t h s -> p (t h s)")
        mem = PRf[:, 0:2048].rearrange("p (t d) -> p t d", t=2)
        memT = kT
        poolm = PRf[:, 2048:4096].rearrange("p (g k s) -> p g k s", g=4, k=2)
        PTf = PT[:].rearrange("p a b -> p (a b)")
        sil = PTf[:, 0:512].rearrange("p (t f) -> p t f", t=2)
        hid = PTf[:, 512:1024].rearrange("p (t f) -> p t f", t=2)
        hidT = PTf[:, 1024:1536].rearrange("p (t f s) -> p t f s", t=2, f=2)
        rt = qiT[:].rearrange("p a s -> p (a s)")
        shared = hT.rearrange("p a s -> p (a s)").rearrange("p (t d) -> p t d", t=2)
        xg = PRf[:, 0:2048].rearrange("p (b d) -> p b d", b=2)
        ysb = PRf[:, 2048:4096].rearrange("p (b d) -> p b d", b=2)
        xT = qT.rearrange("p a s -> p (a s)").rearrange("p (b k w) -> p b k w", b=2, k=8)
        yg = PRf.rearrange("p (b d) -> p b d", b=4)
        max_items = max(ITEMS.values())
        onehot_item = PRf[:, 0:2 * 8 * max_items].rearrange("p (t k i) -> p t k i", t=2, k=8)
        onehot_slot = tmp.rearrange("p t d -> p (t d)").rearrange("p (t k s) -> p t k s", t=2, k=8)
        mixT = PT[:].rearrange("p a b -> p (a b)")[:, 0:1024].rearrange("p (g s) -> p g s", g=4)
        poolw = PT[:].rearrange("p a b -> p (a b)")[:, 1024:1536].rearrange("p (g s) -> p g s", g=4)
        relu = [PRf[:, 0:2048].rearrange("p (h s) -> p h s", h=8), hT]
        ada_rows = Z[:, :, Z1:Z1 + ADA_STEP]
        ada_pairs = [v.rearrange("p a s -> p (a s)").rearrange("p (b n) -> p b n", b=2) for v in (kT, qT)]
        work = yn[:, :, 0:256]
        score = yn[:, :, 256:512]
        mb = PTf[:, 1536:2048].rearrange("p (t s) -> p t s", t=2)
        biasf = bias[:].rearrange("p t h s -> p (t h s)")
        QM = biasf[:, 0:1536].rearrange("p (t n) -> p t n", t=2)
        KM = biasf[:, 1536:3072].rearrange("p (t n) -> p t n", t=2)
        kvm = kmT_vm[:].rearrange("p a s -> p (a s)").rearrange("p (t n) -> p t n", t=2)

        def ada_sum(part):
            if part % 3 == 2:
                return gateB[:, part // 3, :]
            m = part - part // 3
            return biasf[:, m * D:(m + 1) * D]

        def rowv(name):
            a, w = ROW[name]
            return rows[:, a:a + w]

        def copied(engine, key):
            engine.wait_ge(E(f"bank_read_{group_at[key][3]}"), group_at[key][4])

        def slot_of(job):
            seg, j, (_, _, _, n, k) = job_at[job]
            s = j % SLOTS
            return ring[:, 2 * s:2 * s + 2, :].rearrange("p a n -> p (a n)")[:, 0:k * n]\
                .rearrange("p (k n) -> p k n", k=k)

        def last_use(job):
            return max(g[2] for key, g in group_at.items() if key == job or key.startswith(job + "."))

        def loaded_value(job):
            _, j, _ = job_at[job]
            return j % SLOTS, 16 * (j // SLOTS + 1)

        def member_of(n):
            return rt[:, 256:256 + 2 * EXPERTS[n]].rearrange("p (t e) -> p t e", t=2)

        def slabs_of(n):
            return yn[0:EXPERTS[n], 0, 0:2 * P]

        item_column = st[:, 300:302]

        block = ctx.enter_context(nc.Block())

        def moe_weights(n):
            if n == 1:
                return [A[f"expert_w_{w}"][0].rearrange("g e a b -> (g e) a b") for w in ("gate", "up", "down")]
            return [A[f"w_exp_{w}_2"][0] for w in ("gate", "up", "down")]

        def mean_value(name):
            return [n for n in NORMS if n not in X_NORMS].index(name) + 1

        def root_value(name, t=0):
            before = NORMS[:NORMS.index(name)]
            return len(before) + sum(n in X_NORMS for n in before) + t + 1

        def pair_count(engine, n):
            return engine.value_load(pairs_n[0:1, 0:1], min_val=TAKES[n] * S // ROWS_OF[n] // 2, max_val=ITEMS[n] // 2 - 1)

        def ring_gu(s):
            return ring[:, 2 * s:2 * s + 2, :].rearrange("p a n -> p (a n)")\
                .rearrange("p (k n) -> p k n", k=8)

        def ring_down(s):
            return ring[:, 4 + s, :].rearrange("p (k n) -> p k n", k=2)

        @block.sync
        def _(sp):
            def load_job(job):
                seg, j, (name, src, c0, n, k) = job_at[job]
                first = 0 if seg == 0 else n_jobs_one
                if j - first >= SLOTS:
                    sp.wait_ge(E("bank_filled"), last_use(jobs[seg][j - first - SLOTS][0]))
                if job == "shgu":
                    sp.dma_start(slot_of(job)[:, :, 0:FF], A["w_sh_gate_2"][0].rearrange("(k p) n -> p k n", p=P))\
                        .then_inc(E("shared_gate_loaded"), 16)
                    sp.dma_start(slot_of(job)[:, :, FF:2 * FF], A[src][0].rearrange("(k p) n -> p k n", p=P))\
                        .then_inc(E(f"weights_loaded{j % SLOTS}"), 16)
                    return
                sp.dma_start(slot_of(job), A[src][0][:, c0:c0 + n].rearrange("(k p) n -> p k n", p=P))\
                    .then_inc(E(f"weights_loaded{j % SLOTS}"), 16)

            def load(name, dst, src):
                sp.dma_start(dst, src).then_inc(E(name), 16)

            sp.dma_start(x[:], A["x"][0].rearrange("(t p) d -> p t d", p=P)).then_inc(E("x_loaded"), 16)
            for name, n in COLS:
                load("rows_loaded", rowsC[COL[name]:COL[name] + n, :],
                     A[name][0].rearrange("(a b) -> a b", b=P))
            for job in ("z.0", "z.1", "z.2"):
                load_job(job)
            sp.dma_start(mem, A["mem"][0].rearrange("(t p) d -> p t d", p=P)).then_inc(E("mem_loaded"), 16)
            sp.dma_start(rope[:], A["c_rope"].rearrange("(t p) d -> p t d", p=P)).then_inc(E("tables_loaded"), 16)
            sp.dma_start(adm[:], A["c_admissible"].rearrange("(t p) d -> p t d", p=P)).then_inc(E("tables_loaded"), 16)
            sp.dma_start(window[:], A["c_window"]).then_inc(E("tables_loaded"), 16)
            sp.dma_start(lists, A["c_lists"]).then_inc(E("tables_loaded"), 16)
            sp.dma_start(poolm, A["c_pool"].rearrange("g (k p) s -> p g k s", p=P)).then_inc(E("pool_loaded"), 16)
            sp.dma_start(poolw, A["pool_w"][0].rearrange("g c d -> c g d")).then_inc(E("pool_loaded"), 16)
            def ada_pair(i):
                if i >= 2:
                    sp.wait_ge(E("ada_pairs_added"), i - 1)
                part, k = i // 4, 2 * (i % 4)
                sp.dma_start(ada_pairs[i % 2], A["w_ada_2"][0][k * P:(k + 2) * P, part * D:(part + 1) * D].rearrange("(k p) n -> p k n", p=P))\
                    .then_inc(E(f"ada_pair_loaded{i % 2}"), 16)

            ada_pair(0)
            ada_pair(1)
            for n, job in enumerate(jobs[0][3:]):
                load_job(job[0])
                for i in (2 * n + 2, 2 * n + 3):
                    if i < 4 * ADA_DVE:
                        ada_pair(i)
            sp.dma_start(bass.AP(rpb_copies.tensor, 0, [[RPB + 1, 64], [1, RPB]]),
                         bass.AP(A["na_rpb_2"].tensor, 0, [[0, 64], [1, RPB]])).then_inc(E("rpb_copied"), 16)
            sp.dma_start(rw1[:, :, 0:4], A["router_group_w"][0].rearrange("(k p) n -> p k n", p=P)).then_inc(E("router_loaded"), 16)
            sp.dma_start(rw1[:, :, 4:36], A["router_expert_w"][0].rearrange("(k p) n -> p k n", p=P)).then_inc(E("router_loaded"), 16)

            def items(n):
                gate, up, down = moe_weights(n)
                sp.wait_ge(E(f"moe{n}_experts_listed"), 1)
                pairs = pair_count(sp, n)

                def load_pair(i, again):
                    for s in range(2):
                        k = i * 2 + s
                        if again:
                            sp.wait_ge(E(f"moe{n}_gate_up_made"), k)
                            sp.wait_ge(E(f"moe{n}_experts_listed"), 1)
                        elif s == 1:
                            sp.wait_ge(E("bank_filled"), last_use(("wo", "shdown")[n - 1]))
                            sp.wait_ge(E(f"moe{n}_first_rows_asked"), 1)
                            sp.wait_ge(E(f"moe{n}_experts_listed"), 1)
                        e = sp.value_load(item_expert[0:1, bass.ds(k, 1)], min_val=0, max_val=EXPERTS[n] - 1)
                        gu = ring_gu(s)
                        for c0, w in ((0, gate), (FF, up)):
                            sp.dma_start(gu[:, :, c0:c0 + FF], w[bass.ds(e, 1)].rearrange("o (k p) n -> p (o k) n", p=P))\
                                .then_inc(E(f"moe{n}_gate_up_loaded{s}"), 16)
                        if again:
                            sp.wait_ge(E(f"moe{n}_down_made"), k)
                        sp.dma_start(ring_down(s), down[bass.ds(e, 1)].rearrange("o (k p) n -> p (o k) n", p=P))\
                            .then_inc(E(f"moe{n}_down_loaded{s}"), 16)

                load_pair(0, False)
                with sp.Fori(1, pairs) as i:
                    load_pair(i, True)
                return pairs

            def neighbour_bias():
                sp.wait_ge(E("rpb_copied"), 16)
                sp.wait_ge(E("bank_filled"), last_use("mod"))
                for r in range(4):
                    half = 64 * (r % 2)
                    for h in range(HEADS):
                        src = bass.AP(rpb_copies.tensor, h * 465 + (7 - r) * 31 + 15,
                                      [[RPB, 64], [31, 4], [1, 64]])
                        dst = bias[half:half + 64, r // 2, h, :].rearrange("p (a b) -> p a b", a=4)
                        sp.dma_start(dst, src).then_inc(E("bias_loaded"), 16)

            sp.wait_ge(E("xn3_ready"), 2)
            sp.dma_start(xn_dram[1].rearrange("(t p) d -> p t d", p=P), tmp[:]).then_inc(E("xn_stored1"), 16)
            sp.wait_ge(E("bank_filled"), last_use("wo"))
            pairs = items(1)
            for n, job in enumerate(jobs[1]):
                if n < 2:
                    sp.wait_ge(E("moe1_gate_up_made"), pairs * 2 + n)
                elif n == 2:
                    sp.wait_ge(E("moe1_down_made"), pairs * 2 + 1)
                    sp.wait_ge(E("moe1_results_fetched3"), 16)
                load_job(job[0])
                if n == 2:
                    neighbour_bias()
            sp.wait_ge(E("xn5_ready"), 2)
            sp.dma_start(xn_dram[2].rearrange("(t p) d -> p t d", p=P), tmp[:]).then_inc(E("xn_stored2"), 16)
            assert loaded_value("shdown")[0] == 1
            sp.wait_ge(E("bank_filled"), last_use("shgu"))
            items(2)
            for t in range(2):
                sp.wait_ge(E("out_ready"), t + 1)
                sp.dma_start(out[0][t * P:(t + 1) * P, :], x[:, t, :]).then_inc(E("out_stored"), 16)
            sp.wait_ge(E("out_stored"), 32)

        @block.gpsimd
        def _(pool):
            nc.gpsimd.memset(eps[:], EPS).then_inc(E("eps_ready"), 1)
            nc.gpsimd.memset(ones[:], 1.0).then_inc(E("ones_ready"), 1)
            nc.gpsimd.memset(ident[:], 0.0).then_inc(E("ident_zero"), 1)
            pool.wait_ge(E("ident_zero"), 1)
            nc.gpsimd.affine_select(out=ident[:], in_=ident[:], compare_op=ALU.not_equal, fill=1.0, base=0,
                                    pattern=[[-1, P]], channel_multiplier=1).then_inc(E("ident_ready"), 1)
            for name, _ in ROWS:
                pool.dma_start(rowv(name), A[name].rearrange("a n -> (a n)").partition_broadcast(P))\
                    .then_inc(E("gains_loaded"), 16)
            pool.dma_start(earlier[:], A["c_earlier"].rearrange("a n -> (a n)").partition_broadcast(P)).then_inc(E("gains_loaded"), 16)
            pool.dma_start(inv2[:], A["c_inv2"].rearrange("a n -> (a n)").partition_broadcast(P)).then_inc(E("gains_loaded"), 16)
            with nc.allow_non_contiguous_dma("two positions a partition"):
                pool.dma_start(pos_i[:], A["positions_2"].rearrange("a (t p) -> p (a t)", p=P)).then_inc(E("gains_loaded"), 16)
            pool.memset(biasf, 0.0).then_inc(E("ada_cleared"), 1)
            pool.memset(gateB[:], 0.0).then_inc(E("ada_cleared"), 1)
            pieces = [(part, k) for part in range(ADA_DVE, 6) for k in range(KD)]

            def ada_load(q):
                part, k = pieces[q]
                pool.dma_start(ada_rows[:, q % ADA_BUFFERS, :], A["w_ada_2"][0][k * P:(k + 1) * P, part * D:(part + 1) * D])\
                    .then_inc(E(f"ada_loaded{q % ADA_BUFFERS}"), 16)

            for q in range(ADA_BUFFERS):
                ada_load(q)
            pool.wait_ge(E("ada_cleared"), 2)
            for part in range(6):
                pool.dma_start(ada_sum(part)[0:1, :], A["b_ada_2"][:, part * D:(part + 1) * D]).then_inc(E("ada_bias_loaded"), 16)
            pool.wait_ge(E("ada_bias_loaded"), 16 * 6)
            pool.wait_ge(E("silc_ready"), 1)
            for q, (part, k) in enumerate(pieces):
                pool.wait_ge(E(f"ada_loaded{q % ADA_BUFFERS}"), 16 * (q // ADA_BUFFERS + 1))
                w = ada_rows[:, q % ADA_BUFFERS, :]
                pool.tensor_scalar(w, w, silc[:, k:k + 1], None, ALU.mult).then_inc(E("ada_scaled"), 1)
                pool.wait_ge(E("ada_scaled"), q + 1)
                pool.tensor_tensor(ada_sum(part), ada_sum(part), w, ALU.add).then_inc(E("ada_added"), 1)
                pool.wait_ge(E("ada_added"), q + 1)
                if q + ADA_BUFFERS < len(pieces):
                    ada_load(q + ADA_BUFFERS)

            def gathers(n):
                rows_n = ROWS_OF[n]
                pool.wait_ge(E(f"moe{n}_listed"), 1)
                pairs = pair_count(pool, n)
                pool.wait_ge(E(f"xn_stored{n}"), 16)

                def gather(k, slot, taken, count):
                    pool.tensor_copy(token_now[:, slot:slot + 1], token_list[:, bass.ds(k, 1)]).then_inc(E(f"moe{n}_{taken}"), 1)
                    pool.wait_ge(E(f"moe{n}_listed"), 1)
                    pool.wait_ge(E(f"moe{n}_{taken}"), count)
                    pool.indirect_dma_start(xg[0:rows_n, slot, :], None, xn_dram[n],
                                            bass.IndirectOffsetOnAxis(ap=token_now[0:rows_n, slot:slot + 1], axis=0))\
                        .then_inc(E(f"moe{n}_rows_fetched{slot}"), 16)

                gather(0, 0, "first_tokens_taken", 1)
                pool.sem_inc(E(f"moe{n}_first_rows_asked"), 1)
                with pool.Fori(1, pairs + 1) as i:
                    for s in range(2):
                        j = i * 2 - 2 + s
                        pool.wait_ge(E(f"moe{n}_rows_turned"), j + 1)
                        pool.wait_ge(E(f"moe{n}_listed"), 1)
                        gather(j + 1, 1 - s, f"tokens_taken{1 - s}", i)
                pool.wait_ge(E(f"moe{n}_stored"), 1)
                for q in range(2 * TAKES[n]):
                    t, k = q // TAKES[n], q % TAKES[n]
                    if q >= 4:
                        pool.wait_ge(E(f"moe{n}_rows_added"), q - 3)
                    pool.indirect_dma_start(yg[:, q % 4, :], None, y_dram[n][0:S * TAKES[n], :],
                                            bass.IndirectOffsetOnAxis(ap=y_rows[:, t, k:k + 1], axis=0))\
                        .then_inc(E(f"moe{n}_results_fetched{q % 4}"), 16)

            gathers(1)
            gathers(2)

        GAINS = 16 * (len(ROWS) + 3)

        @block.tensor
        def _(pe):
            made = [0]

            def opened(key):
                seg, n, value, reader, _ = group_at[key]
                assert value == made[0] + 1, key
                if n >= 8:
                    _, _, _, r8, v8 = group_at[groups[seg][n - 8][0]]
                    pe.wait_ge(E(f"bank_read_{r8}"), v8)
                return bank[:, n % 8, :]

            def closed(ins):
                made[0] += 1
                ins.then_inc(E("bank_filled"), 1)

            def linear(key, job, lhs, t, c0=0, n=None):
                b = opened(key)
                _, _, (_, _, _, width, nk) = job_at[job]
                n = n or width
                w = slot_of(job)
                s, v = loaded_value(job)
                pe.wait_ge(E(f"weights_loaded{s}"), v)
                for k in range(nk):
                    mm = nc.tensor.matmul(b[:, 0:n], lhs(k, t), w[:, k, c0:c0 + n], start=(k == 0), stop=(k == nk - 1))
                closed(mm)

            def tok(src):
                return lambda k, t: src[:, k, t * P:(t + 1) * P]

            def turn(key, pieces, rows_=P):
                b = opened(key)
                for j, piece in enumerate(pieces):
                    m = piece.shape[-1]
                    tr = nc.tensor.transpose(b[0:m, j * P:(j + 1) * P], piece, ident[:])
                closed(tr)

            def turn_x(name, src, ready):
                for t in range(2):
                    pe.wait_ge(E(ready), t + 1)
                    for half in range(2):
                        turn(f"{name}.{2 * t + half}", [src[:, t, (4 * half + j) * P:(4 * half + j + 1) * P] for j in range(4)])

            def attend(name, q, k, v, heads, dk, dv, nkeys, per_bank, paired):
                vparts = dv
                for t in range(2):
                    nk = nkeys[t]
                    for i, hs in enumerate(score_heads(heads, nk, paired)):
                        b = opened(f"{name}.s.{t}.{i}")
                        for j, h in enumerate(hs):
                            mm = nc.tensor.matmul(b[:, j * nk:(j + 1) * nk], q(h, t), k(h, nk), start=True, stop=True)
                        closed(mm)
                for t in range(2):
                    nk = nkeys[t]
                    pieces = [(h, kt) for h in range(heads) for kt in range(nk // P)]
                    pe.wait_ge(E(f"{name}_probs{t}"), 1)
                    for i in range(len(pieces) // 4):
                        turn(f"{name}.p.{t}.{i}", [PR[:, t, h, kt * P:(kt + 1) * P] for h, kt in pieces[4 * i:4 * i + 4]])
                    copied(pe, f"{name}.p.{t}.{len(pieces) // 4 - 1}")
                    b = opened(f"{name}.o.{t}")
                    for n, (h, kt) in enumerate(pieces):
                        mm = nc.tensor.matmul(b[:, h * dv:(h + 1) * dv], PT[:, n, :], v(h, kt),
                                              start=(kt == 0), stop=(kt == nk // P - 1))
                    closed(mm)
                for t in range(2):
                    copied(pe, f"{name}.o.{t}")
                    turn(f"{name}.yT.{t}", [yn[:, t, j * P:(j + 1) * P] for j in range(4)])

            def pair(src):
                return lambda h, t: src[64 * (h % 2):64 * (h % 2) + 64, h // 2, t * P:(t + 1) * P]

            def pair_keys(src):
                return lambda h, nk: src[64 * (h % 2):64 * (h % 2) + 64, h // 2, 0:nk]

            def routing(n):
                experts_n = EXPERTS[n]
                member = member_of(n)
                pe.wait_ge(E(f"moe{n}_members_ready"), 1)
                b = opened(f"rank{n}")
                nc.tensor.matmul(b[:, 0:experts_n], tri, member[:, 0, :], start=True, stop=True)
                nc.tensor.matmul(b[:, experts_n:2 * experts_n], ones[:], member[:, 0, :], start=True, stop=False)
                nc.tensor.matmul(b[:, experts_n:2 * experts_n], tri, member[:, 1, :], start=False, stop=True)
                for t in range(2):
                    mm = nc.tensor.matmul(b[0:experts_n, 2 * experts_n:2 * experts_n + 1], member[:, t, :], ones[:, 0:1],
                                          start=(t == 0), stop=(t == 1))
                closed(mm)
                pe.wait_ge(E(f"moe{n}_slabs_ready"), 1)
                b = opened(f"start{n}")
                for a in range(2):
                    mm = nc.tensor.matmul(b[:, a * P:a * P + experts_n + 1], slabs_of(n)[:, a * P:(a + 1) * P],
                                          order[0:experts_n, 0:experts_n + 1], start=True, stop=True)
                closed(mm)

            def experts_turned(n):
                pe.wait_ge(E(f"moe{n}_item_column_ready"), 1)
                b = opened(f"items{n}")
                for a in range(2):
                    mm = nc.tensor.matmul(b[0:1, a * P:(a + 1) * P], item_column[:, a:a + 1], ident[:], start=True, stop=True)
                closed(mm)

            def tokens_listed(n):
                pe.wait_ge(E(f"moe{n}_onehots_ready"), 1)
                b = opened(f"tokens{n}")
                pieces = [(t, k) for t in range(2) for k in range(TAKES[n])]
                for q, (t, k) in enumerate(pieces):
                    mm = nc.tensor.matmul(b[:, 0:ITEMS[n]], onehot_slot[:, t, k, :], onehot_item[:, t, k, 0:ITEMS[n]],
                                          start=(q == 0), stop=(q == len(pieces) - 1))
                closed(mm)

            def items(n):
                rows_n = ROWS_OF[n]
                pe.wait_ge(E(f"moe{n}_listed"), 1)
                pairs = pair_count(pe, n)

                def turn_rows(slot, fetched):
                    pe.wait_ge(E(f"moe{n}_rows_fetched{slot}"), fetched)
                    for k in range(KD):
                        tr = nc.tensor.transpose(bank[:, 4 + k // 4, (k % 4) * P:(k % 4 + 1) * P], xg[:, slot, k * P:(k + 1) * P], ident[:])
                    tr.then_inc(E(f"moe{n}_rows_turned"), 1)

                def down(s, j):
                    pe.wait_ge(E(f"moe{n}_hidden_copied"), j + 1)
                    pe.wait_ge(E(f"moe{n}_result_copied"), j + 1)
                    for half in range(2):
                        for f in range(2):
                            mm = nc.tensor.matmul(bank[0:rows_n, half, :], hidT[:, s, f, 0:rows_n],
                                                  ring_down(s)[:, f, half * 512:(half + 1) * 512], start=(f == 0), stop=(f == 1))
                    mm.then_inc(E(f"moe{n}_down_made"), 1)

                turn_rows(0, 16)
                pe.wait_ge(E(f"moe{n}_down_loaded1"), 16)
                with pe.Fori(0, pairs) as i:
                    for s in range(2):
                        j = i * 2 + s
                        pe.wait_ge(E(f"moe{n}_rows_copied"), j + 1)
                        pe.wait_ge(E(f"moe{n}_gate_up_loaded{s}"), i * 32 + 32)
                        for k in range(KD):
                            mm = nc.tensor.matmul(bank[0:rows_n, 2, :], xT[:, s, k, 0:rows_n], ring_gu(s)[:, k, :],
                                                  start=(k == 0), stop=(k == KD - 1))
                        mm.then_inc(E(f"moe{n}_gate_up_made"), 1)
                        turn_rows(1 - s, i * 16 + 16 * (s + 1))
                        if s == 1:
                            pe.wait_ge(E(f"moe{n}_down_loaded0"), i * 16 + 16)
                        down(1 - s, j)
                        pe.wait_ge(E(f"moe{n}_hidden_made"), j + 1)
                        for f in range(2):
                            tr = nc.tensor.transpose(bank[:, 3, f * P:(f + 1) * P], hid[:, s, f * P:(f + 1) * P], ident[:])
                        tr.then_inc(E(f"moe{n}_hidden_turned"), 1)
                    pe.wait_ge(E(f"moe{n}_down_loaded1"), i * 16 + 16)
                down(1, pairs * 2)
                pe.wait_ge(E(f"moe{n}_stored"), 1)

            pe.wait_ge(E("ident_ready"), 1)
            pe.wait_ge(E("rows_loaded"), 16 * len(COLS))
            b = opened("cols")
            closed(nc.tensor.transpose(b[:, 0:N_COLS], rowsC[0:N_COLS, :], ident[0:N_COLS, 0:N_COLS]))
            turn_x("xT1", tmp, "xn1_ready")
            copied(pe, "xT1.3")
            for c in range(6):
                if c == 4:
                    turn_x("memT", mem, "memn_ready")
                for t in range(2):
                    linear(f"z.{c}.{t}", f"z.{c}", tok(hT), t)
            pe.wait_ge(E("ki_ready"), 1)
            turn("kiT", [tmp[:, t, 0:P] for t in range(2)])
            pe.wait_ge(E("qi_ready"), 1)
            for t in range(2):
                turn(f"qiT.{t}", [Z[:, t, QI0 + j * P:QI0 + (j + 1) * P] for j in range(4)])
            copied(pe, "qiT.1")
            i = 0
            for t in range(2):
                nk = (t + 1) * P
                for hs in score_heads(HEADS, nk, True):
                    b = opened(f"idx.{i}")
                    for j, h in enumerate(hs):
                        half = 64 * (h % 2)
                        mm = nc.tensor.matmul(b[:, j * nk:(j + 1) * nk], pair(qiT)(h, t), kiT[half:half + 64, 0:nk], start=True, stop=True)
                    closed(mm)
                    i += 1
            copied(pe, "memT.3")
            for c in range(2):
                for t in range(2):
                    linear(f"kv.{c}.{t}", f"kv.{c}", tok(memT), t)
            pe.wait_ge(E("pool_loaded"), 32)
            for g2 in range(2):
                b = opened(f"mixT.{g2}")
                for j in range(2):
                    g = 2 * g2 + j
                    for k in range(2):
                        mm = nc.tensor.matmul(b[:, j * S:(j + 1) * S], Z[:, k, U0 + g * P:U0 + (g + 1) * P], poolm[:, g, k, :],
                                              start=(k == 0), stop=(k == 1))
                closed(mm)
            copied(pe, "mixT.1")
            for g2 in range(2):
                b = opened(f"ypT.{g2}")
                for j in range(2):
                    g = 2 * g2 + j
                    mm = nc.tensor.matmul(b[:, j * S:(j + 1) * S], poolw[:, g, :], mixT[:, g, :], start=True, stop=True)
                closed(mm)
            for a, c0 in (("q", Q0), ("k", K0)):
                pe.wait_ge(E(f"{a}_ready"), 1)
                for t in range(2):
                    turn(f"{a}T.{t}", [Z[:, t, c0 + j * P:c0 + (j + 1) * P] for j in range(4)])
            pe.wait_ge(E("km_ready"), 1)
            for t in range(2):
                turn(f"kmT.{t}", [yT[:].rearrange("p a s -> p (a s)")[:, 1024 + t * 512 + j * P:1024 + t * 512 + (j + 1) * P] for j in range(4)])
            copied(pe, "kmT.1")
            attend("dsa", pair(qT), pair_keys(kT), lambda h, kt: Z[:, kt, V0 + h * HD:V0 + (h + 1) * HD],
                   HEADS, HD, HD, (P, S), 4, True)
            copied(pe, "dsa.yT.1")
            copied(pe, "ypT.1")
            for n in range(2):
                for t in range(2):
                    linear(f"wout.{n}.{t}", f"wout.{n}", tok(yT), t)
            turn_x("xT2", tmp, "xn2_ready")
            copied(pe, "xT2.3")
            for t in range(2):
                linear(f"wq.{t}", "wq", tok(hT), t)
            pe.wait_ge(E("qm_ready"), 1)
            for t in range(2):
                turn(f"qmT.{t}", [Z[:, t, j * P:(j + 1) * P] for j in range(4)])
            copied(pe, "qmT.1")
            attend("mem", lambda h, t: qT[:, h, t * P:(t + 1) * P], lambda h, nk: kmT[:, h, 0:nk],
                   lambda h, kt: vm[:, kt, h * XD:(h + 1) * XD], XH, XD, XD, (S, S), 2, False)
            copied(pe, "mem.yT.1")
            for n in range(2):
                for t in range(2):
                    linear(f"wo.{n}.{t}", "wo", tok(yT), t, c0=512 * n, n=512)
            turn_x("xT3", tmp, "xn3_ready")
            copied(pe, "xT3.3")
            pe.wait_ge(E("router_loaded"), 32)
            for t in range(2):
                b = opened(f"route1.{t}")
                for k in range(KD):
                    mm = nc.tensor.matmul(b[:, 0:36], tok(hT)(k, t), rw1[:, k, :], start=(k == 0), stop=(k == KD - 1))
                closed(mm)
            routing(1)
            experts_turned(1)
            pe.wait_ge(E("ada_added"), (6 - ADA_DVE) * KD)
            pe.wait_ge(E("ada_pairs_added"), 4 * ADA_DVE)
            b = opened("mod")
            for m, part in enumerate((0, 1, 3, 4)):
                for k in range(KD):
                    mm = nc.tensor.matmul(b[:, m * 8 + k:m * 8 + k + 1], ada_sum(part)[:, k * P:(k + 1) * P], ones[:, 0:1], start=True, stop=True)
            closed(mm)
            tokens_listed(1)
            for i in range(4):
                b = opened(f"gate.{i}")
                half = (i % 2) * 512
                closed(nc.tensor.matmul(b, ones[:], gateB[:, i // 2, half:half + 512], start=True, stop=True))
            copied(pe, "gate.3")
            items(1)

            turn_x("xT4", tmp, "xn4_ready")
            pe.wait_ge(E("xT4_ready"), 1)
            for c in range(8):
                for t in range(2):
                    linear(f"y.{c}.{t}", f"y.{c}", tok(hT), t)
            for a, c0 in (("nq", NQ0), ("nk", NK0)):
                pe.wait_ge(E(f"{a}_ready"), 1)
                for t in range(2):
                    turn(f"{a}T.{t}", [Z[:, t, c0 + j * P:c0 + (j + 1) * P] for j in range(4)])
            copied(pe, "nkT.1")
            attend("na", pair(qT), pair_keys(kT), lambda h, kt: Z[:, kt, NV0 + h * HD:NV0 + (h + 1) * HD],
                   HEADS, HD, HD, (S, S), 4, True)
            pe.wait_ge(E("lat_ready"), 1)
            for t in range(2):
                turn(f"qlT.{t}", [Z[:, t, QL0 + j * P:QL0 + (j + 1) * P] for j in range(2)])
            turn("klT", [Z[:, t, KL0:KL0 + P] for t in range(2)])
            copied(pe, "klT")
            for t in range(2):
                for c in range(2):
                    linear(f"uq.{c}.{t}", "uq", tok(qiT), t, c0=384 * c, n=384)
            for t in range(2):
                for c in range(2):
                    linear(f"ukv.{c}.{t}", "ukv", lambda k, t: kiT[:, t * P:(t + 1) * P], t, c0=512 * c, n=512)
            copied(pe, "na.yT.1")
            for n in range(2):
                for t in range(2):
                    linear(f"pna.{n}.{t}", "pna", tok(yT), t, c0=512 * n, n=512)
            for a, src in (("mq", QM), ("mk", KM)):
                pe.wait_ge(E(f"{a}_ready"), 1)
                for t in range(2):
                    for i in range(2):
                        turn(f"{a}T.{t}.{i}", [src[:, t, (4 * i + j) * QK:(4 * i + j + 1) * QK] for j in range(4)])
            copied(pe, "mkT.1.1")
            attend("mla", lambda h, t: qT[0:QK, h, t * P:(t + 1) * P], lambda h, nk: kT[0:QK, h, 0:nk],
                   lambda h, kt: kvm[:, kt, h * 128 + 64:h * 128 + 128], HEADS, QK, HD, (S, S), 2, False)
            copied(pe, "mla.yT.1")
            for n in range(2):
                for t in range(2):
                    linear(f"pmla.{n}.{t}", "pmla", lambda k, t: yT[:, 4 + k, t * P:(t + 1) * P], t, c0=512 * n, n=512)
            turn_x("mgT", Z[:, :, GN0:GN0 + D], "merged_ready")
            copied(pe, "mgT.3")
            for n in range(2):
                for t in range(2):
                    linear(f"wout2.{n}.{t}", f"wout2.{n}", tok(hT), t)
            turn_x("xT5", tmp, "xn5_ready")
            pe.wait_ge(E("xT5_ready"), 1)
            for t in range(2):
                linear(f"route2.{t}", "route2", tok(hT), t)
            pe.wait_ge(E("shared_gate_loaded"), 16)
            for t in range(2):
                linear(f"shgu.{t}", "shgu", tok(hT), t)

            for t in range(2):
                pe.wait_ge(E("shared_hidden_ready"), t + 1)
                turn(f"shT.{t}", [hid[:, t, f * P:(f + 1) * P] for f in range(2)])
            copied(pe, "shT.1")
            for n in range(2):
                for t in range(2):
                    linear(f"shdown.{n}.{t}", "shdown", lambda k, t: hidT[:, t, k, :], t, c0=512 * n, n=512)
            routing(2)
            experts_turned(2)
            tokens_listed(2)
            copied(pe, "shdown.1.1")
            items(2)

        @block.scalar
        def _(act):
            def arrived(key):
                seg, n, value, reader, _ = group_at[key]
                assert reader == "act", key
                act.wait_ge(E("bank_filled"), value)
                return bank[:, n % 8, :]

            def drained(ins):
                ins.then_inc(E("bank_read_act"), 1)

            reads = [0]

            def copy(key, dst, src=None, func=ACT.Copy, scale=1.0):
                b = arrived(key)
                src = b[:, 0:dst.free_size()] if src is None else src(b)
                drained(nc.scalar.activation(dst, src, func, scale=scale))
                assert group_at[key][4] == reads[0] + 1, key
                reads[0] += 1

            def flat(b, n, w):
                return b[:, 0:n * w].rearrange("p (n w) -> p n w", n=n)

            def root(name, ap):
                act.wait_ge(E("mean_squares_ready"), mean_value(name))
                nc.scalar.activation(ap, ap, ACT.Sqrt).then_inc(E("roots_ready"), 1)

            def norm_x(name, dst):
                for t in range(2):
                    if name == "x1":
                        act.wait_ge(E("x_loaded"), 16)
                        act.wait_ge(E("eps_ready"), 1)
                    else:
                        act.wait_ge(E("x_added"), 2 * (X_NORMS.index(name) - 1) + t + 1)
                    s = st[:, t:t + 1]
                    nc.scalar.activation(dst[:, t, :], x[:, t, :], ACT.Square, accum_out=s).then_inc(E("squares_summed"), 1)
                    act.wait_ge(E("squares_summed"), 2 * X_NORMS.index(name) + t + 1)
                    nc.scalar.activation(s, s, ACT.Sqrt, bias=eps[:], scale=1.0 / D).then_inc(E("roots_ready"), 1)

            def turned4(key, dst):
                copy(key, dst, lambda b: flat(b, 4, P))

            def attend(name, heads, nkeys, dst):
                for t in range(2):
                    nk = nkeys[t]
                    act.wait_ge(E(f"{name}_scored{t}"), 1)
                    for h in range(heads):
                        ins = nc.scalar.activation(PR[:, t, h, 0:nk], PR[:, t, h, 0:nk], ACT.Exp, bias=st[:, 400 + 8 * t + h:401 + 8 * t + h],
                                                   accum_out=st[:, 416 + 8 * t + h:417 + 8 * t + h])
                    ins.then_inc(E(f"{name}_probs{t}"), 1)
                    if t == 1:
                        act.wait_ge(E("bank_filled"), group_at[f"{name}.o.0"][2])
                    for i in range(heads * (nk // P) // 4):
                        copy(f"{name}.p.{t}.{i}", PT[:, 4 * i:4 * i + 4, :], lambda b: flat(b, 4, P))
                for t in range(2):
                    turned4(f"{name}.yT.{t}", dst[:, :, t * P:(t + 1) * P])

            def items(n):
                rows_n = ROWS_OF[n]
                act.wait_ge(E(f"moe{n}_listed"), 1)
                pairs = pair_count(act, n)

                def results(j, slot, stored, stored_before):
                    act.wait_ge(E(f"moe{n}_down_made"), j + 1)
                    act.wait_ge(E(f"moe{n}_result_stored{slot}"), stored)
                    for half in range(2):
                        ins = nc.scalar.activation(ysb[0:rows_n, slot, half * 512:(half + 1) * 512], bank[0:rows_n, half, :], ACT.Copy)
                    ins.then_inc(E(f"moe{n}_result_copied"), 1)
                    act.wait_ge(E(f"moe{n}_result_copied"), j + 2)
                    act.wait_ge(E(f"moe{n}_result_stored{1 - slot}"), stored_before)
                    act.wait_ge(E(f"moe{n}_listed"), 1)
                    base = act.value_load(item_base[0:1, bass.ds(j, 1)], min_val=0, max_val=S * TAKES[n])
                    act.dma_start(y_dram[n][bass.ds(base, rows_n)], ysb[0:rows_n, slot, :])\
                        .then_inc(E(f"moe{n}_result_stored{slot}"), 16)

                with act.Fori(0, pairs) as i:
                    for s in range(2):
                        j = i * 2 + s
                        act.wait_ge(E(f"moe{n}_gate_up_made"), j + 2)
                        nc.scalar.activation(sil[0:rows_n, s, :], bank[0:rows_n, 2, 0:FF], ACT.Silu).then_inc(E(f"moe{n}_silu_made"), 1)
                        results(j, s, i * 16 + 16, i * 16 + 16 * (s + 1))
                        act.wait_ge(E(f"moe{n}_hidden_turned"), j + 1)
                        nc.scalar.activation(hidT[:, s, :, 0:rows_n], bank[:, 3, 0:2 * P].rearrange("p (a b) -> p a b", a=2)[:, :, 0:rows_n], ACT.Copy)\
                            .then_inc(E(f"moe{n}_hidden_copied"), 1)
                results(pairs * 2, 0, pairs * 16 + 16, pairs * 16 + 16)
                act.wait_ge(E(f"moe{n}_result_stored0"), pairs * 16 + 32)
                act.wait_ge(E(f"moe{n}_result_stored1"), pairs * 16 + 16)
                act.sem_inc(E(f"moe{n}_stored"), 1)

            norm_x("x1", tmp)
            copied(act, "cols")
            nc.scalar.activation(silc[:], cols[:, COL["c_2"]:COL["c_2"] + 8], ACT.Silu).then_inc(E("silc_ready"), 1)
            zc = dict(enumerate(Z_CHUNKS))
            for c in range(6):
                for t in range(2):
                    copy(f"z.{c}.{t}", Z[:, t, zc[c][0]:zc[c][0] + zc[c][1]])
                    if (c, t) == (5, 0):
                        root("front", st[:, 4:4 + 34])
                if c == 0:
                    root("mem", st[:, 2:4])
            copy("kiT", kiT[:], )
            for t in range(2):
                turned4(f"qiT.{t}", qiT[:, :, t * P:(t + 1) * P])
            i = 0
            for t in range(2):
                nk = (t + 1) * P
                for hs in score_heads(HEADS, nk, True):
                    copy(f"idx.{i}", relu[t][:, hs[0]:hs[-1] + 1:2, 0:nk], lambda b: flat(b, len(hs), nk), ACT.Relu)
                    i += 1
            for c in range(2):
                for t in range(2):
                    dst = yT[:].rearrange("p a s -> p (a s)")[:, 1024 + t * 512:1536 + t * 512] if c == 0 else vm[:, t, :]
                    copy(f"kv.{c}.{t}", dst)
            for g2 in range(2):
                copy(f"mixT.{g2}", mixT[:, 2 * g2:2 * g2 + 2, :], lambda b: flat(b, 2, S))
            for a, dst in (("q", qT), ("k", kT)):
                for t in range(2):
                    turned4(f"{a}T.{t}", dst[:, 0:4, t * P:(t + 1) * P])
            root("km", st[:, 60:68])
            for t in range(2):
                turned4(f"kmT.{t}", kmT[:, :, t * P:(t + 1) * P])
            attend("dsa", HEADS, (P, S), yT[:, 4:8, :])
            norm_x("x2", tmp)
            for t in range(2):
                copy(f"wq.{t}", Z[:, t, 0:512])
            root("qm", st[:, 60:68])
            for t in range(2):
                turned4(f"qmT.{t}", qT[:, 0:4, t * P:(t + 1) * P])
            attend("mem", XH, (S, S), yT[:, 0:4, :])
            norm_x("x3", tmp)
            act.wait_ge(E("route1_shifted"), 1)
            nc.scalar.activation(rt[:, 0:8], rt[:, 0:8], ACT.Exp).then_inc(E("route1_exps"), 1)
            nc.scalar.activation(rt[:, 8:24], rt[:, 8:24], ACT.Exp).then_inc(E("route1_exps"), 1)
            nc.scalar.activation(rt[:, 24:26], rt[:, 24:26], ACT.Exp).then_inc(E("route1_exps"), 1)
            act.wait_ge(E("angles_ready"), 1)
            nc.scalar.activation(trig[:, 0:2, :, :], trig[:, 0:2, :, :], ACT.Sin).then_inc(E("trig_ready"), 1)
            copy("mod", modc[:])
            for i in range(4):
                copy(f"gate.{i}", gateB[:, i // 2, (i % 2) * 512:(i % 2 + 1) * 512])
            items(1)
            norm_x("x4", tmp)
            for c in range(8):
                c0, w = Y_CHUNKS[c]
                for t in range(2):
                    copy(f"y.{c}.{t}", Z[:, t, c0:c0 + w])
            root("nqk", st[:, 4:4 + 36])
            for a, dst in (("nq", qT), ("nk", kT)):
                for t in range(2):
                    turned4(f"{a}T.{t}", dst[:, 0:4, t * P:(t + 1) * P])
            for t in range(2):
                nc.scalar.activation(Z[:, t, GN0:Z2], Z[:, t, GN0:Z2], ACT.Sigmoid).then_inc(E("sigmoids_ready"), 1)
            attend("na", HEADS, (S, S), yT[:, 0:4, :])
            for t in range(2):
                copy(f"qlT.{t}", qiT[:, 0:2, t * P:(t + 1) * P], lambda b: flat(b, 2, P))
            copy("klT", kiT[:])
            for t in range(2):
                for c in range(2):
                    copy(f"uq.{c}.{t}", QM[:, t, 384 * c:384 * (c + 1)])
            for t in range(2):
                for c in range(2):
                    copy(f"ukv.{c}.{t}", kvm[:, t, 512 * c:512 * (c + 1)])
            for a in range(2):
                root(("mq", "mk")[a], st[:, 100 + 16 * a:116 + 16 * a])
            for a, dst in (("mq", qT), ("mk", kT)):
                for t in range(2):
                    for i in range(2):
                        copy(f"{a}T.{t}.{i}", dst[0:QK, 4 * i:4 * i + 4, t * P:(t + 1) * P],
                             lambda b: b[0:QK, :].rearrange("p (n w) -> p n w", n=4))
            attend("mla", HEADS, (S, S), yT[:, 4:8, :])
            for i in range(4):
                t, half = i // 2, i % 2
                turned4(f"mgT.{i}", hT[:, 4 * half:4 * half + 4, t * P:(t + 1) * P])
            norm_x("x5", tmp)
            act.wait_ge(E("route2_logits"), 1)
            nc.scalar.activation(rt[:, 0:128], rt[:, 0:128], ACT.Sigmoid).then_inc(E("route2_scores"), 1)
            for t in range(2):
                act.wait_ge(E("bank_filled"), group_at[f"shgu.{t}"][2])
                nc.scalar.activation(sil[:, t, :], bank[:, group_at[f"shgu.{t}"][1] % 8, 0:FF], ACT.Silu).then_inc(E("shared_silu_made"), 1)
            for t in range(2):
                copy(f"shT.{t}", hidT[:, t, :, :], lambda b: flat(b, 2, P))
            for n in range(2):
                for t in range(2):
                    copy(f"shdown.{n}.{t}", shared[:, t, n * 512:(n + 1) * 512])
            items(2)

        @block.vector
        def _(dve):
            V = nc.vector
            chain = [0]

            def link(ins):
                chain[0] += 1
                ins.then_inc(E("dve_step"), 1)
                dve.wait_ge(E("dve_step"), chain[0])

            def signal(name):
                dve.sem_inc(E(name), 1)

            def arrived(key):
                seg, n, value, reader, _ = group_at[key]
                assert reader == "dve", key
                dve.wait_ge(E("bank_filled"), value)
                return bank[:, n % 8, :]

            reads = [0]

            def drained(ins, key):
                assert group_at[key][4] == reads[0] + 1, key
                reads[0] += 1
                ins.then_inc(E("bank_read_dve"), 1)

            def settled():
                dve.wait_ge(E("bank_read_dve"), reads[0])

            def flat(b, n, w):
                return b[:, 0:n * w].rearrange("p (n w) -> p n w", n=n)

            def over(ap, shape):
                return ap.broadcast_to(shape)

            def mean_square(src, square, out_, width):
                link(V.tensor_tensor(square, src, src, ALU.mult))
                link(V.tensor_reduce(out_, square, X, ALU.add))
                link(V.tensor_scalar(out_, out_, 1.0 / width, EPS, ALU.mult, ALU.add))

            def inverse(name, ap):
                link(V.reciprocal(ap, ap))
                signal("mean_squares_ready")
                dve.wait_ge(E("roots_ready"), root_value(name))

            def norm_x(name, src, dst):
                s = st[:, 0:2]
                for t in range(2):
                    dve.wait_ge(E("roots_ready"), root_value(name, t))
                    link(V.reciprocal(s[:, t:t + 1], s[:, t:t + 1]))
                    link(V.tensor_scalar(dst[:, t, :], src[:, t, :], s[:, t:t + 1], None, ALU.mult))
                    signal(f"{name.replace('x', 'xn')}_ready")

            def evacuate_T(name, dst, gain, shift=None):
                for i in range(4):
                    t, half = i // 2, i % 2
                    key = f"{name}.{i}"
                    b = arrived(key)
                    o = dst[:, 4 * half:4 * half + 4, t * P:(t + 1) * P]
                    if shift is None:
                        g = over(gain[:, 4 * half:4 * half + 4].unsqueeze(2), [P, 4, P])
                        drained(V.tensor_tensor(o, flat(b, 4, P), g, ALU.mult), key)
                    else:
                        for j in range(4):
                            k = 4 * half + j
                            ins = V.tensor_scalar(o[:, j, :], b[:, j * P:(j + 1) * P], gain[:, k:k + 1], shift[:, k:k + 1], ALU.mult, ALU.add)
                        drained(ins, key)
                settled()
                if shift is not None:
                    signal(f"{name}_ready")

            def heads_of(ap, h, w):
                return ap.rearrange("p t (h w) -> p t h w", h=h)

            def scaled(ap, inv, gain, h, w):
                link(V.tensor_tensor(ap, ap, over(inv.unsqueeze(3), [P, 2, h, w]), ALU.mult))
                link(V.tensor_tensor(ap, ap, over(gain.unsqueeze(1).unsqueeze(1), [P, 2, h, w]), ALU.mult))

            def roped(ap, h):
                t1 = heads_of(tmp[:, :, 0:h * HD], h, HD)
                t2 = heads_of(tmp[:, :, 512:512 + h * HD], h, HD)
                c = over(rope[:, :, 0:64].unsqueeze(2), [P, 2, h, 64])
                V.tensor_tensor(t1, ap, c, ALU.mult)
                V.tensor_tensor(t2[:, :, :, 0:32], ap[:, :, :, 32:64], over(rope[:, :, 64:96].unsqueeze(2), [P, 2, h, 32]), ALU.mult)
                link(V.tensor_tensor(t2[:, :, :, 32:64], ap[:, :, :, 0:32], over(rope[:, :, 96:128].unsqueeze(2), [P, 2, h, 32]), ALU.mult))
                link(V.tensor_tensor(ap, t1, t2, ALU.add))

            def attend(name, heads, nkeys, dv, scale, paired, biased):
                for t in range(2):
                    nk = nkeys[t]
                    for i, hs in enumerate(score_heads(heads, nk, paired)):
                        key = f"{name}.s.{t}.{i}"
                        b = flat(arrived(key), len(hs), nk)
                        step = hs[1] - hs[0]
                        o = PR[:, t, hs[0]:hs[-1] + 1:step, 0:nk]
                        if biased is None:
                            drained(V.tensor_scalar(o, b, scale, None, ALU.mult), key)
                        else:
                            drained(V.scalar_tensor_tensor(o, b, scale, biased(t, hs, nk), ALU.mult, ALU.add), key)
                    settled()
                    link(V.tensor_reduce(st[:, 400 + 8 * t:400 + 8 * t + heads], PR[:, t, 0:heads, 0:nk], X, ALU.max, negate=True))
                    signal(f"{name}_scored{t}")
                for t in range(2):
                    key = f"{name}.o.{t}"
                    b = flat(arrived(key), heads, dv)
                    inv = st[:, 416 + 8 * t:416 + 8 * t + heads]
                    link(V.reciprocal(inv, inv))
                    if t == 0 and name == "mla":
                        copied(dve, "na.yT.1")
                    drained(V.tensor_tensor(yn[:, t, :].rearrange("p (h w) -> p h w", h=heads), b,
                                            over(inv.unsqueeze(2), [P, heads, dv]), ALU.mult), key)

            def gated(name, g0):
                for n in range(2):
                    for t in range(2):
                        key = f"{name}.{n}.{t}"
                        b = arrived(key)
                        o = Z[:, t, g0 + n * 512:g0 + (n + 1) * 512]
                        drained(V.tensor_tensor(o, b, o, ALU.mult), key)

            def add_to_x(name, gate=None):
                for n in range(2):
                    for t in range(2):
                        key = f"{name}.{n}.{t}"
                        b = arrived(key)
                        o = x[:, t, n * 512:(n + 1) * 512]
                        if gate is None:
                            drained(V.tensor_tensor(o, b, o, ALU.add), key)
                            if n == 1:
                                settled()
                        else:
                            tg = tmp[:, t, n * 512:(n + 1) * 512]
                            drained(V.tensor_tensor(tg, b, gate[:, n * 512:(n + 1) * 512], ALU.mult), key)
                            settled()
                            link(V.tensor_tensor(o, tg, o, ALU.add))
                        if n == 1:
                            signal("x_added")
                settled()

            def ranks(values, groups_, n, out_, scratch):
                v = values
                a = over(v.unsqueeze(3), [P, groups_, n, n])
                b = over(v.unsqueeze(2), [P, groups_, n, n])
                sc = [s[:, 0:groups_ * n * n].rearrange("p (g i j) -> p g i j", g=groups_, i=n) for s in scratch]
                e = over(earlier[:].rearrange("p (i j) -> p i j", i=8)[:, 0:n, 0:n].unsqueeze(1), [P, groups_, n, n])
                V.tensor_tensor(sc[0], b, a, ALU.is_gt)
                link(V.tensor_tensor(sc[1], b, a, ALU.is_equal))
                link(V.tensor_tensor(sc[1], sc[1], e, ALU.mult))
                link(V.tensor_tensor(sc[0], sc[0], sc[1], ALU.add))
                link(V.tensor_reduce(out_, sc[0], X, ALU.add))

            def starts(n):
                e_n, r_n, k_n = EXPERTS[n], ROWS_OF[n], TAKES[n]
                signal(f"moe{n}_members_ready")
                ynf = yn.rearrange("p t n -> p (t n)")
                place = ynf[:, 2 * P:2 * P + 2 * e_n].rearrange("p (t e) -> p t e", t=2)
                key = f"rank{n}"
                b = arrived(key)
                count = st[0:e_n, 303:304]
                link(V.tensor_copy(count, b[0:e_n, 2 * e_n:2 * e_n + 1]))
                drained(V.tensor_copy(place, b[:, 0:2 * e_n].rearrange("p (t e) -> p t e", t=2)), key)
                settled()
                slabs = st[0:e_n, 302:303]
                link(V.tensor_scalar(slabs, count, 0.0, None, ALU.is_gt))
                for k in range(1, S // r_n):
                    link(V.tensor_scalar(st[0:e_n, 304:305], count, float(k * r_n), None, ALU.is_gt))
                    link(V.tensor_tensor(slabs, slabs, st[0:e_n, 304:305], ALU.add))
                link(V.tensor_copy(slabs_of(n)[:, 0:P], over(slabs, [e_n, P])))
                link(V.tensor_copy(slabs_of(n)[:, P:2 * P], over(count, [e_n, P])))
                signal(f"moe{n}_slabs_ready")
                key = f"start{n}"
                b = arrived(key)
                starts_ = ynf[:, 3 * P + 64:3 * P + 64 + 2 * (e_n + 1)].rearrange("p (a e) -> p a e", a=2)
                start, first_row = starts_[:, 0, :], starts_[:, 1, :]
                drained(V.tensor_copy(starts_, b[:, 0:2 * P].rearrange("p (a e) -> p a e", a=2)[:, :, 0:e_n + 1]), key)
                settled()
                before = ynf[:, 6 * P:6 * P + e_n]
                ends = ynf[:, 6 * P + 64:6 * P + 64 + e_n]
                link(V.tensor_tensor(before, start[:, 1:e_n + 1], over(tok_id[:, 0:1], [P, e_n]), ALU.is_le))
                link(V.tensor_reduce(item_column[:, 0:1], before, X, ALU.add))
                link(V.tensor_scalar(item_column[:, 0:1], item_column[:, 0:1], float(e_n - 1), None, ALU.min))
                for a in range(2):
                    link(V.tensor_tensor(ends, before, starts_[:, a, 1:e_n + 1], ALU.mult))
                    link(V.tensor_reduce(st[:, 306 + a:307 + a], ends, X, ALU.max))
                link(V.tensor_tensor(st[:, 306:307], tok_id[:, 0:1], st[:, 306:307], ALU.subtract))
                link(V.scalar_tensor_tensor(item_column[:, 1:2], st[:, 306:307], float(r_n), st[:, 307:308], ALU.mult, ALU.add))
                link(V.tensor_scalar(item_column[:, 1:2], item_column[:, 1:2], float(S * k_n), None, ALU.min))
                signal(f"moe{n}_item_column_ready")
                half = st[0:1, 305:306]
                link(V.tensor_scalar(half, start[0:1, e_n:e_n + 1], 0.5, 0.25, ALU.mult, ALU.add))
                link(V.tensor_scalar(half, half, MAGIC, None, ALU.add))
                link(V.tensor_scalar(half, half, MAGIC, None, ALU.subtract))
                link(V.tensor_copy(pairs_n, half))
                key = f"items{n}"
                b = arrived(key)
                link(V.memset(item_base[0:1, 0:1], 0))
                link(V.tensor_copy(item_base[0:1, 1:P + 1], b[0:1, P:2 * P]))
                drained(V.tensor_copy(item_expert[0:1, :], b[0:1, 0:P]), key)
                settled()
                signal(f"moe{n}_experts_listed")
                member = member_of(n)
                out_place = rt[:, 384:384 + 2 * e_n].rearrange("p (t e) -> p t e", t=2)
                link(V.tensor_tensor(out_place, place, over(first_row[:, 0:e_n].unsqueeze(1), [P, 2, e_n]), ALU.add))
                link(V.tensor_scalar(start, start, float(r_n), 1.0, ALU.mult, ALU.add))
                link(V.tensor_tensor(place, place, over(start[:, 0:e_n].unsqueeze(1), [P, 2, e_n]), ALU.add))
                link(V.tensor_tensor(place, place, member, ALU.mult))
                top = st[:, 310:326].rearrange("p (t k) -> p t k", t=2)
                for t in range(2):
                    link(V.max(top[:, t, :], place[:, t, :]))
                row, item, slot = [st[:, c:c + 16].rearrange("p (t k) -> p t k", t=2) for c in (326, 342, 358)]
                link(V.tensor_scalar(row, top, 1.0, None, ALU.subtract))
                link(V.tensor_scalar(item, row, 1.0 / r_n, 0.5 / r_n - 0.5, ALU.mult, ALU.add))
                link(V.tensor_scalar(item, item, MAGIC, None, ALU.add))
                link(V.tensor_scalar(item, item, MAGIC, None, ALU.subtract))
                link(V.scalar_tensor_tensor(slot, item, -float(r_n), row, ALU.mult, ALU.add))
                i_n = ITEMS[n]
                for t in range(2):
                    o = onehot_item[:, t, 0:k_n, 0:i_n]
                    link(V.tensor_tensor(o, over(iota[:, 0:i_n].unsqueeze(1), [P, k_n, i_n]), over(item[:, t, 0:k_n].unsqueeze(2), [P, k_n, i_n]), ALU.is_equal))
                    link(V.tensor_scalar(o, o, tok_id[:, t:t + 1], None, ALU.mult))
                return slot

            def shares(n):
                e_n, k_n = EXPERTS[n], TAKES[n]
                kTf = kT.rearrange("p a s -> p (a s)")
                place = yn.rearrange("p t n -> p (t n)")[:, 2 * P:2 * P + 2 * e_n].rearrange("p (t e) -> p t e", t=2)
                out_place = rt[:, 384:384 + 2 * e_n].rearrange("p (t e) -> p t e", t=2)
                top = st[:, 310:326].rearrange("p (t k) -> p t k", t=2)
                same = kTf[:, 0:2 * k_n * e_n].rearrange("p (t k e) -> p t k e", t=2, k=k_n)
                same_row = kTf[:, D:D + 2 * k_n * e_n].rearrange("p (t k e) -> p t k e", t=2, k=k_n)
                wide = [P, k_n, e_n]
                for t in range(2):
                    link(V.tensor_tensor(same[:, t], over(place[:, t, :].unsqueeze(1), wide), over(top[:, t, 0:k_n].unsqueeze(2), wide), ALU.is_equal))
                    link(V.tensor_tensor(same_row[:, t], same[:, t], over(out_place[:, t, :].unsqueeze(1), wide), ALU.mult))
                    link(V.tensor_tensor(same[:, t], same[:, t], over(gates[:, t, 0:e_n].unsqueeze(1), wide), ALU.mult))
                link(V.tensor_reduce(share[:, :, 0:k_n], same, X, ALU.add))
                row = st[:, 326:326 + 2 * k_n].rearrange("p (t k) -> p t k", t=2)
                link(V.tensor_reduce(row, same_row, X, ALU.add))
                link(V.tensor_copy(y_rows[:, :, 0:k_n], row))

            def lists_taken(n, slot):
                for t in range(2):
                    k_n = TAKES[n]
                    link(V.tensor_tensor(onehot_slot[:, t, 0:k_n], over(iota.unsqueeze(1), [P, k_n, P]), over(slot[:, t, 0:k_n].unsqueeze(2), [P, k_n, P]), ALU.is_equal))
                signal(f"moe{n}_onehots_ready")
                key = f"tokens{n}"
                b = arrived(key)
                drained(V.tensor_copy(token_list[:, 0:ITEMS[n]], b[:, 0:ITEMS[n]]), key)
                settled()

            def items(n, gain, shift, gate):
                rows_n = ROWS_OF[n]
                V.memset(hidT[:, 1, :, :], 0.0)
                if rows_n < P:
                    V.memset(hid[rows_n:P], 0.0)
                    V.memset(xg[rows_n:P], 0.0)
                link(V.memset(hidT[:, 0, :, :], 0.0))
                dve.sem_inc(E(f"moe{n}_rows_turned"), 1)
                dve.sem_inc(E(f"moe{n}_gate_up_made"), 1)
                dve.sem_inc(E(f"moe{n}_hidden_copied"), 1)
                dve.sem_inc(E(f"moe{n}_result_copied"), 1)
                dve.sem_inc(E(f"moe{n}_result_stored0"), 16)
                dve.sem_inc(E(f"moe{n}_result_stored1"), 16)
                signal(f"moe{n}_listed")
                pairs = pair_count(dve, n)
                shares(n)

                def take_rows(slot):
                    if shift is None:
                        for half in range(2):
                            ins = V.tensor_tensor(xT[:, slot, 4 * half:4 * half + 4, 0:rows_n], flat(bank[:, 4 + half, :], 4, P)[:, :, 0:rows_n],
                                                  over(gain[:, 4 * half:4 * half + 4].unsqueeze(2), [P, 4, rows_n]), ALU.mult)
                    else:
                        for k in range(KD):
                            ins = V.tensor_scalar(xT[:, slot, k, 0:rows_n], bank[:, 4 + k // 4, (k % 4) * P:(k % 4) * P + rows_n],
                                                  gain[:, k:k + 1], shift[:, k:k + 1], ALU.mult, ALU.add)
                    ins.then_inc(E(f"moe{n}_rows_copied"), 1)

                dve.wait_ge(E(f"moe{n}_rows_turned"), 2)
                take_rows(0)
                with dve.Fori(0, pairs) as i:
                    for s in range(2):
                        j = i * 2 + s
                        dve.wait_ge(E(f"moe{n}_silu_made"), j + 1)
                        V.tensor_tensor(hid[0:rows_n, s, :], bank[0:rows_n, 2, FF:2 * FF], sil[0:rows_n, s, :], ALU.mult)\
                            .then_inc(E(f"moe{n}_hidden_made"), 1)
                        dve.wait_ge(E(f"moe{n}_rows_turned"), j + 3)
                        take_rows(1 - s)
                for q in range(2 * TAKES[n]):
                    t, k = q // TAKES[n], q % TAKES[n]
                    dve.wait_ge(E(f"moe{n}_results_fetched{q % 4}"), 16 * (q // 4 + 1))
                    w = share[:, t, k:k + 1]
                    o = x[:, t, :] if gate is None else shared[:, t, :]
                    if k >= 1:
                        dve.wait_ge(E(f"moe{n}_rows_added"), q)
                    ins = V.scalar_tensor_tensor(o, yg[:, q % 4, :], w, o, ALU.mult, ALU.add)
                    ins.then_inc(E(f"moe{n}_rows_added"), 1)
                    if k == TAKES[n] - 1:
                        dve.wait_ge(E(f"moe{n}_rows_added"), q + 1)
                        if gate is not None:
                            link(V.tensor_tensor(o, o, gate, ALU.mult))
                            link(V.tensor_tensor(x[:, t, :], o, x[:, t, :], ALU.add))
                            signal("out_ready")
                        else:
                            signal("x_added")

            link(V.memset(gates[:], 0.0))
            dve.wait_ge(E("x_loaded"), 16)
            norm_x("x1", x, tmp)
            b = arrived("cols")
            drained(V.tensor_copy(cols[:, 0:N_COLS], b[:, 0:N_COLS]), "cols")
            settled()

            def col(name):
                return cols[:, COL[name]:COL[name] + 8]

            evacuate_T("xT1", hT, col("mix_norm"))

            def ada_added(i):
                dve.wait_ge(E(f"ada_pair_loaded{i % 2}"), 16 * (i // 2 + 1))
                for b in range(2):
                    part, k = i // 4, 2 * (i % 4) + b
                    link(V.scalar_tensor_tensor(ada_sum(part), ada_pairs[i % 2][:, b, :], silc[:, k:k + 1], ada_sum(part), ALU.mult, ALU.add))
                signal("ada_pairs_added")

            dve.wait_ge(E("mem_loaded"), 16)
            mean_square(mem, tmp, st[:, 2:4], D)
            inverse("mem", st[:, 2:4])
            for t in range(2):
                link(V.tensor_scalar(mem[:, t, :], mem[:, t, :], st[:, 2 + t:3 + t], None, ALU.mult))
            dve.sem_inc(E("memn_ready"), 2)
            ms = st[:, 4:38].rearrange("p (t h) -> p t h", t=2)
            dve.wait_ge(E("gains_loaded"), GAINS)
            dve.wait_ge(E("tables_loaded"), 64)
            link(V.tensor_copy(pos_f[:], pos_i[:]))
            ang, ang2, red, wrap = trig[:, 0], trig[:, 1], trig[:, 2], trig[:, 3]
            for t in range(2):
                link(V.tensor_scalar(ang[:, t, :], inv2[:], pos_f[:, t:t + 1], None, ALU.mult))
            link(V.tensor_scalar(red, ang, 1.0 / TWO_PI, MAGIC, ALU.mult, ALU.add))
            link(V.tensor_scalar(red, red, MAGIC, None, ALU.subtract))
            link(V.tensor_scalar(wrap, ang, 1.0 / TWO_PI, 0.25, ALU.mult, ALU.add))
            link(V.tensor_scalar(wrap, wrap, MAGIC, None, ALU.add))
            link(V.tensor_scalar(wrap, wrap, MAGIC, None, ALU.subtract))
            link(V.tensor_scalar(wrap, wrap, 0.25, None, ALU.subtract))
            link(V.tensor_copy(ang2, ang))
            for c in TWO_PI_PARTS:
                link(V.scalar_tensor_tensor(ang, red, -c, ang, ALU.mult, ALU.add))
                link(V.scalar_tensor_tensor(ang2, wrap, -c, ang2, ALU.mult, ALU.add))
            link(V.tensor_scalar(trig[:, 0:2], trig[:, 0:2], PI_IN, -PI_IN, ALU.min, ALU.max))
            signal("angles_ready")
            dve.wait_ge(E("ada_bias_loaded"), 16 * 6)
            dve.wait_ge(E("silc_ready"), 1)
            ada_added(0)
            ada_added(1)
            copied(dve, "z.1.1")
            mean_square(Z[:, :, KI0:KI0 + 64], tmp[:, :, 0:64], st[:, 38:40], HD)
            copied(dve, "z.0.1")
            roped(heads_of(Z[:, :, QI0:QI0 + 512], 8, HD), 8)
            signal("qi_ready")
            ada_added(2)
            ada_added(3)
            for a, c, c0 in ((0, 2, Q0), (1, 3, K0)):
                copied(dve, f"z.{c}.1")
                mean_square(heads_of(Z[:, :, c0:c0 + 512], 8, HD), heads_of(tmp[:, :, 0:512], 8, HD), ms[:, :, 8 * a:8 * a + 8], HD)
                ada_added(4 + 2 * a)
                ada_added(5 + 2 * a)
            link(V.tensor_copy(ms[:, :, 16:17].rearrange("p t h -> p (t h)"), st[:, 38:40]))
            evacuate_T("memT", memT, col("mem_norm"))
            inverse("front", st[:, 4:38])
            ki = heads_of(Z[:, :, KI0:KI0 + 64], 1, HD)
            scaled(ki, ms[:, :, 16:17], rowv("idx_k_norm"), 1, HD)
            roped(ki, 1)
            V.tensor_copy(tmp[:, :, 0:64], Z[:, :, KI0:KI0 + 64])
            link(V.tensor_copy(tmp[:, :, 64:128], Z[:, :, KI0:KI0 + 64]))
            signal("ki_ready")
            copied(dve, "qiT.1")
            for a, c0, g in ((0, Q0, "q_norm"), (1, K0, "k_norm")):
                ap = heads_of(Z[:, :, c0:c0 + 512], 8, HD)
                scaled(ap, ms[:, :, 8 * a:8 * a + 8], rowv(g), 8, HD)
                roped(ap, 8)
                signal("qk"[a] + "_ready")
            for t in range(2):
                nk = (t + 1) * P
                copied(dve, f"idx.{1 + 4 * t}")
                for h in range(HEADS):
                    w = Z[:, t, WI0 + h:WI0 + h + 1]
                    if h == 0:
                        link(V.tensor_scalar(score[:, t, 0:nk], relu[t][:, h, 0:nk], w, None, ALU.mult))
                    else:
                        link(V.scalar_tensor_tensor(score[:, t, 0:nk], relu[t][:, h, 0:nk], w, score[:, t, 0:nk], ALU.mult, ALU.add))
                link(V.scalar_tensor_tensor(work[:, t, 0:nk], score[:, t, 0:nk], IDX_SCALE, adm[:, t, 0:nk], ALU.mult, ALU.add))
                for r in range(TOPK_KEYS // 8):
                    link(V.max(st[:, 80:88], work[:, t, 0:nk]))
                    link(V.match_replace(work[:, t, 0:nk], st[:, 80:88], work[:, t, 0:nk], -FLT))
                link(V.tensor_scalar(mb[:, t, 0:nk], work[:, t, 0:nk], -1e38, -BIG, ALU.is_gt, ALU.mult))
            copied(dve, "kv.1.1")
            km = yT[:].rearrange("p a s -> p (a s)")[:, 1024:2048].rearrange("p (t h w) -> p t h w", t=2, h=4)
            kms = st[:, 60:68].rearrange("p (t h) -> p t h", t=2)
            kmq = heads_of(tmp[:, :, 512:1024], 4, XD)
            mean_square(km, kmq, kms, XD)
            inverse("km", st[:, 60:68])
            scaled(km, kms, rowv("xattn_k_norm"), 4, XD)
            signal("km_ready")
            for g2 in range(2):
                key = f"ypT.{g2}"
                b = arrived(key)
                ps = cols[:, COL["pool_scale"] + 2 * g2:COL["pool_scale"] + 2 * g2 + 2]
                drained(V.tensor_tensor(yT[:, 2 * g2:2 * g2 + 2, :], flat(b, 2, S), over(ps.unsqueeze(2), [P, 2, S]), ALU.mult), key)
            settled()
            attend("dsa", HEADS, (P, S), HD, HD ** -0.5, True,
                   lambda t, hs, nk: over(mb[:, t, 0:nk].unsqueeze(1), [P, len(hs), nk]))
            add_to_x("wout")
            norm_x("x2", x, tmp)
            evacuate_T("xT2", hT, col("xattn_norm"))
            copied(dve, "wq.1")
            qm = heads_of(Z[:, :, 0:512], 4, XD)
            mean_square(qm, heads_of(tmp[:, :, 0:512], 4, XD), kms, XD)
            inverse("qm", st[:, 60:68])
            scaled(qm, kms, rowv("xattn_q_norm"), 4, XD)
            signal("qm_ready")
            attend("mem", XH, (S, S), XD, XD ** -0.5, False, None)
            add_to_x("wo")
            norm_x("x3", x, tmp)
            evacuate_T("xT3", hT, col("ffn_norm"))
            gl = rt[:, 0:8].rearrange("p (t g) -> p t g", t=2)
            ein = rt[:, 8:24].rearrange("p (t e) -> p t e", t=2)
            dif = rt[:, 24:26]
            el = rt[:, 32:96].rearrange("p (t e) -> p t e", t=2)
            oh = rt[:, 96:104].rearrange("p (t g) -> p t g", t=2)
            rk = rt[:, 104:120].rearrange("p (t e) -> p t e", t=2)
            m8 = rt[:, 120:136].rearrange("p (t e) -> p t e", t=2)
            mx = rt[:, 136:138]
            gw = rt[:, 138:140]
            mul = rt[:, 140:204].rearrange("p (t e) -> p t e", t=2)
            scratch = [rt[:, 256:384], rt[:, 384:512]]
            for t in range(2):
                key = f"route1.{t}"
                b = arrived(key)
                V.tensor_tensor(gl[:, t, :], b[:, 0:4], rowv("router_group_b"), ALU.add)
                drained(V.tensor_tensor(el[:, t, :], b[:, 4:36], rowv("router_expert_b"), ALU.add), key)
            settled()
            ranks(gl, 2, 4, oh, scratch)
            link(V.tensor_scalar(oh, oh, 0.5, None, ALU.is_lt))
            link(V.tensor_reduce(mx, gl, X, ALU.max))
            link(V.tensor_tensor(gl, gl, over(mx.unsqueeze(2), [P, 2, 4]), ALU.subtract))
            link(V.tensor_tensor(mul.rearrange("p t (g e) -> p t g e", g=4), el.rearrange("p t (g e) -> p t g e", g=4),
                                 over(oh.unsqueeze(3), [P, 2, 4, 8]), ALU.mult))
            link(V.tensor_reduce(ein, mul.rearrange("p t (g e) -> p t e g", g=4), X, ALU.add))
            for t in range(2):
                link(V.max(m8[:, t, :], ein[:, t, :]))
            ranks(ein, 2, 8, rk, scratch)
            link(V.tensor_scalar(rk, rk, 1.5, None, ALU.is_lt))
            for t in range(2):
                link(V.tensor_tensor(member_of(1)[:, t, :].rearrange("p (g e) -> p g e", g=4),
                                     over(rk[:, t, :].unsqueeze(1), [P, 4, 8]), over(oh[:, t, :].unsqueeze(2), [P, 4, 8]), ALU.mult))
            link(V.tensor_tensor(ein, ein, over(m8[:, :, 0:1], [P, 2, 8]), ALU.subtract))
            link(V.tensor_tensor(dif, m8[:, :, 1:2].squeeze(2), m8[:, :, 0:1].squeeze(2), ALU.subtract))
            signal("route1_shifted")
            dve.wait_ge(E("route1_exps"), 3)
            link(V.tensor_reduce(gw, gl, X, ALU.add))
            link(V.tensor_scalar(dif, dif, 1.0, None, ALU.add))
            link(V.tensor_tensor(gw, gw, dif, ALU.mult))
            link(V.reciprocal(gw, gw))
            link(V.tensor_tensor(rk, rk, ein, ALU.mult))
            link(V.tensor_tensor(rk, rk, over(gw.unsqueeze(2), [P, 2, 8]), ALU.mult))
            for t in range(2):
                link(V.tensor_tensor(gates[:, t, 0:E1].rearrange("p (g e) -> p g e", g=4),
                                     over(rk[:, t, :].unsqueeze(1), [P, 4, 8]), over(oh[:, t, :].unsqueeze(2), [P, 4, 8]), ALU.mult))
            slot = starts(1)
            dve.wait_ge(E("xn_stored1"), 16)
            lists_taken(1, slot)
            items(1, col("ffn_norm"), None, None)

            copied(dve, "mod")
            for m, g in ((0, "g_norm1_2"), (1, "g_norm2_2")):
                link(V.tensor_scalar(gs4[:, 8 * m:8 * m + 8], modc[:, 16 * m + 8:16 * m + 16], 1.0, None, ALU.add))
                link(V.tensor_tensor(gs4[:, 8 * m:8 * m + 8], gs4[:, 8 * m:8 * m + 8], col(g), ALU.mult))
            norm_x("x4", x, tmp)
            evacuate_T("xT4", hT, gs4[:, 0:8], modc[:, 0:8])
            dve.wait_ge(E("bias_loaded"), 16 * 4 * HEADS)
            for t in range(2):
                o = bias[:, t, :, :].rearrange("p h (r c) -> p (h r) c", c=64)
                link(V.tensor_tensor(o, o, over(window[:].unsqueeze(1), [P, 32, 64]), ALU.add))
            nms = st[:, 4:36].rearrange("p (t h) -> p t h", t=2)
            for a, c0 in ((0, NQ0), (1, NK0)):
                copied(dve, f"y.{a}.1")
                mean_square(heads_of(Z[:, :, c0:c0 + 512], 8, HD), heads_of(tmp[:, :, 0:512], 8, HD), nms[:, :, 8 * a:8 * a + 8], HD)
            copied(dve, "y.3.1")
            mean_square(Z[:, :, QL0:QL0 + 256], tmp[:, :, 0:256], st[:, 36:38], 256)
            mean_square(Z[:, :, KL0:KL0 + 128], tmp[:, :, 0:128], st[:, 38:40], 128)
            inverse("nqk", st[:, 4:40])
            for a, c0, g in ((0, NQ0, "g_na_q_2"), (1, NK0, "g_na_k_2")):
                scaled(heads_of(Z[:, :, c0:c0 + 512], 8, HD), nms[:, :, 8 * a:8 * a + 8], rowv(g), 8, HD)
                signal(f"n{'qk'[a]}_ready")
            scaled(heads_of(Z[:, :, QL0:QL0 + 256], 1, 256), st[:, 36:38].unsqueeze(2), rowv("g_q_lat_2"), 1, 256)
            scaled(heads_of(Z[:, :, KL0:KL0 + 128], 1, 128), st[:, 38:40].unsqueeze(2), rowv("g_kv_lat_2"), 1, 128)
            signal("lat_ready")
            attend("na", HEADS, (S, S), HD, HD ** -0.5, True, lambda t, hs, nk: bias[:, t, hs[0]:hs[-1] + 1:2, :])
            sin, cos = trig[:, 0], trig[:, 1]
            dve.wait_ge(E("trig_ready"), 1)

            def rotate(ap, h):
                lo, hi = ap[:, :, :, 0:16], ap[:, :, :, 16:32]
                s = over(sin.unsqueeze(2), [P, 2, h, 16])
                c = over(cos.unsqueeze(2), [P, 2, h, 16])
                q = [tmp[:, :, 128 * i:128 * i + 16 * h].rearrange("p t (h w) -> p t h w", h=h) for i in range(4)]
                V.tensor_tensor(q[0], lo, c, ALU.mult)
                V.tensor_tensor(q[1], hi, s, ALU.mult)
                V.tensor_tensor(q[2], hi, c, ALU.mult)
                link(V.tensor_tensor(q[3], lo, s, ALU.mult))
                V.tensor_tensor(lo, q[0], q[1], ALU.subtract)
                link(V.tensor_tensor(hi, q[2], q[3], ALU.add))

            kr = heads_of(Z[:, :, KR0:KR0 + 32], 1, 32)
            rotate(kr, 1)
            mms = st[:, 100:132].rearrange("p (a t h) -> p a t h", a=2, t=2)
            QMh, KMh = heads_of(QM, 8, QK), heads_of(KM, 8, QK)
            copied(dve, "uq.1.1")
            rotate(QMh[:, :, :, 64:96], 8)
            mean_square(QMh, heads_of(tmp[:, :, 0:768], 8, QK), mms[:, 0], QK)
            inverse("mq", st[:, 100:116])
            scaled(QMh, mms[:, 0], rowv("g_mla_q_2"), 8, QK)
            signal("mq_ready")
            copied(dve, "ukv.1.1")
            for t in range(2):
                V.tensor_copy(KMh[:, t, :, 0:64], kvm[:, t, :].rearrange("p (h w) -> p h w", h=8)[:, :, 0:64])
                link(V.tensor_copy(KMh[:, t, :, 64:96], over(Z[:, t, KR0:KR0 + 32].unsqueeze(1), [P, 8, 32])))
            mean_square(KMh, heads_of(tmp[:, :, 0:768], 8, QK), mms[:, 1], QK)
            inverse("mk", st[:, 116:132])
            scaled(KMh, mms[:, 1], rowv("g_mla_k_2"), 8, QK)
            signal("mk_ready")
            dve.wait_ge(E("sigmoids_ready"), 2)
            gated("pna", GN0)
            attend("mla", HEADS, (S, S), HD, QK ** -0.5, False, None)
            gated("pmla", GM0)
            settled()
            link(V.tensor_tensor(Z[:, :, GN0:GN0 + D], Z[:, :, GN0:GN0 + D], Z[:, :, GM0:GM0 + D], ALU.add))
            dve.sem_inc(E("merged_ready"), 2)
            copied(dve, "gate.3")
            add_to_x("wout2", gateB[:, 0, :])
            norm_x("x5", x, tmp)
            evacuate_T("xT5", hT, gs4[:, 8:16], modc[:, 16:24])
            sc = rt[:, 0:128].rearrange("p (t e) -> p t e", t=2)
            for t in range(2):
                key = f"route2.{t}"
                b = arrived(key)
                drained(V.tensor_copy(sc[:, t, :], b[:, 0:E2]), key)
            settled()
            signal("route2_logits")
            for t in range(2):
                key = f"shgu.{t}"
                b = arrived(key)
                dve.wait_ge(E("shared_silu_made"), t + 1)
                drained(V.tensor_tensor(hid[:, t, :], b[:, FF:2 * FF], sil[:, t, :], ALU.mult), key)
                settled()
                signal("shared_hidden_ready")
            dve.wait_ge(E("route2_scores"), 1)
            sel = rt[:, 128:256].rearrange("p (t e) -> p t e", t=2)
            link(V.tensor_tensor(sel, sc, over(rowv("e_bias_2").unsqueeze(1), [P, 2, E2]), ALU.add))
            t8 = yn[:, 0, 0:128].rearrange("p (t g e) -> p t g e", t=2, g=8)
            for t in range(2):
                for g in range(G2):
                    V.max(t8[:, t, g, :], sel[:, t, 8 * g:8 * g + 8])
            gsum = yn[:, 0, 128:144].rearrange("p (t g) -> p t g", t=2)
            link(V.memset(yn[:, 0, 144:146], 0.0))
            link(V.tensor_tensor(gsum, t8[:, :, :, 0:1].squeeze(3), t8[:, :, :, 1:2].squeeze(3), ALU.add))
            grank = yn[:, 0, 160:176].rearrange("p (t g) -> p t g", t=2)
            ranks(gsum, 2, 8, grank, [yn[:, 0, 256:384], yn[:, 0, 384:512]])
            link(V.tensor_scalar(grank, grank, 3.5, -BIG, ALU.is_gt, ALU.mult))
            link(V.tensor_tensor(sel.rearrange("p t (g e) -> p t g e", g=8), sel.rearrange("p t (g e) -> p t g e", g=8),
                                 over(grank.unsqueeze(3), [P, 2, 8, 8]), ALU.add))
            for t in range(2):
                link(V.max(t8[:, t, 0, :], sel[:, t, :]))
                link(V.match_replace(sel[:, t, :], t8[:, t, 0, :], sel[:, t, :], -FLT))
            link(V.tensor_scalar(member_of(2), sel, -1e38, None, ALU.is_lt))
            link(V.tensor_tensor(sel, member_of(2), sc, ALU.mult))
            link(V.tensor_reduce(st[:, 0:2], sel, X, ALU.add))
            link(V.reciprocal(st[:, 0:2], st[:, 0:2]))
            for t in range(2):
                link(V.tensor_scalar(gates[:, t, 0:E2], sel[:, t, :], st[:, t:t + 1], 2.5, ALU.mult, ALU.mult))
            slot = starts(2)
            dve.wait_ge(E("xn_stored2"), 16)
            lists_taken(2, slot)
            items(2, gs4[:, 8:16], modc[:, 16:24], gateB[:, 1, :])


IDX_SCALE = (64 ** -0.5) * (8 ** -0.5)
MAGIC = float(1.5 * 2 ** 23)
PI_IN = 3.1415925
TWO_PI_PARTS = (6.28125, 0.0019350051879882812, 3.019916050e-07)


def score_heads(heads, nk, paired):
    per = 512 // nk
    order = [h for parity in range(2) for h in range(parity, heads, 2)] if paired else list(range(heads))
    return [order[i:i + per] for i in range(0, heads, per)]


INPUTS = ['x', 'mem', 'mix_norm', 'w_in', 'pool_w', 'pool_scale', 'q_norm', 'k_norm', 'idx_k_norm', 'w_out',
          'xattn_norm', 'mem_norm', 'xattn_wq', 'xattn_wkv', 'xattn_q_norm', 'xattn_k_norm', 'xattn_wo',
          'ffn_norm', 'router_group_w', 'router_group_b', 'router_expert_w', 'router_expert_b',
          'expert_w_gate', 'expert_w_up', 'expert_w_down', 'c_2', 'positions_2', 'w_ada_2', 'b_ada_2',
          'g_norm1_2', 'w_in_2', 'g_na_q_2', 'g_na_k_2', 'na_rpb_2', 'g_q_lat_2', 'w_uq_2', 'g_kv_lat_2',
          'w_ukv_2', 'g_mla_q_2', 'g_mla_k_2', 'w_proj_na_2', 'w_proj_mla_2', 'w_out_2', 'g_norm2_2',
          'w_router_2', 'e_bias_2', 'w_exp_gate_2', 'w_exp_up_2', 'w_exp_down_2', 'w_sh_gate_2',
          'w_sh_up_2', 'w_sh_down_2']


def kernel(**inputs):
    from concourse import bacc
    from concourse.bass_utils import run_bass_kernel_spmd

    nc = bacc.Bacc("TRN2", target_bir_lowering=False, num_devices=1)
    arrays, A = {}, {}
    data = {name: np.ascontiguousarray(inputs[name]) for name in INPUTS}
    data.update(shape_constants())
    for name, a in data.items():
        arrays[f"in_{name}"] = a
        A[name] = nc.dram_tensor(f"in_{name}", a.shape, mybir.dt.from_np(a.dtype), kind="ExternalInput").ap()
    out = nc.dram_tensor("out", (1, S, D), F32, kind="ExternalOutput").ap()
    build_program(nc, A, out)
    r = run_bass_kernel_spmd(nc, [arrays], core_ids=[0])
    return r.results[0]["out"]
```
